# Optimizing a Trainium2 kernel written in Bass

```python
import math
import jax
import jax.numpy as jnp
from jax import lax
import numpy as np

D_MODEL = 1024
BATCH = 1
SEQ = 512
DEPTH = 2
DEC_BATCH = 8
DEC_SEQ = 8
PAST_LEN = 1024
PAGE_SIZE = 128

N_A_LAYERS = (DEPTH + 1) // 2
N_C_LAYERS = DEPTH // 2
MIX_WIDTH = D_MODEL
S5_WIDTH = MIX_WIDTH // 2
S5_GROUP = 16
S5_GROUPS = S5_WIDTH // S5_GROUP
S5_STATE = 64
S5_DT_MIN = 0.001
S5_DT_MAX = 0.1
MOBA_HEADS = 8
MOBA_HEAD_DIM = (MIX_WIDTH - S5_WIDTH) // MOBA_HEADS
MOBA_BLOCK = 256
MOBA_TOPK = 3
MOBA_QCHUNK = 16
ROPE_THETA = 500000.0
ROPE_DIM = MOBA_HEAD_DIM // 4
HGRN_WIDTH = MIX_WIDTH // 2
HGRN_HEADS = 4
HGRN_HEAD_DIM = HGRN_WIDTH // HGRN_HEADS
HGRN_CHUNK = 64
SB_HEADS = 8
SB_HEAD_DIM = (MIX_WIDTH - HGRN_WIDTH) // SB_HEADS
SB_QBLOCK = 128
IN_A = S5_WIDTH + 3 * MOBA_HEADS * MOBA_HEAD_DIM
IN_C = 4 * HGRN_WIDTH + 3 * SB_HEADS * SB_HEAD_DIM
D_FF = 2816
CONV_W = 3
PLE_DIM = 256
POOL_NUM = 5
POOL_DEN = 4
EPS = 1e-6
NEG = -1e30

kernel_name = 'hybrid_s5_moba_hgrn2_stickbreak_step'

def rmsnorm(x, g):
    xf = x.astype(jnp.float32)
    y = xf * lax.rsqrt(jnp.mean(xf * xf, axis=-1, keepdims=True) + EPS)
    return (y * g.astype(jnp.float32)).astype(x.dtype)

def partial_rope(x, pos):
    half = ROPE_DIM // 2
    inv = ROPE_THETA ** (-jnp.arange(half, dtype=jnp.float32) / half)
    ang = pos.astype(jnp.float32)[:, None] * inv[None, :]
    cos = jnp.cos(ang)[None, :, None, :]
    sin = jnp.sin(ang)[None, :, None, :]
    xf = x.astype(jnp.float32)
    x1 = xf[..., :half]
    x2 = xf[..., half:ROPE_DIM]
    out = jnp.concatenate([x1 * cos - x2 * sin, x2 * cos + x1 * sin, xf[..., ROPE_DIM:]], axis=-1)
    return out.astype(x.dtype)

def _cmul(ar, ai, br, bi):
    return ar * br - ai * bi, ar * bi + ai * br

def _ssm_combine(e1, e2):
    a1r, a1i, b1r, b1i = e1
    a2r, a2i, b2r, b2i = e2
    ar, ai = _cmul(a2r, a2i, a1r, a1i)
    br, bi = _cmul(a2r, a2i, b1r, b1i)
    return ar, ai, br + b2r, bi + b2i

def s5_mixer(u, h0_re, h0_im, a_re, a_im, log_dt, b_re, b_im, c_re, c_im, d, w_glu, b_glu):
    f32 = jnp.float32
    bsz, t, _ = u.shape
    uf = u.astype(f32).reshape(bsz, t, S5_GROUPS, S5_GROUP)
    ar = a_re.astype(f32)
    ai = a_im.astype(f32)
    dt = jnp.exp(log_dt.astype(f32))[:, None]
    mag = jnp.exp(ar * dt)
    abr = mag * jnp.cos(ai * dt)
    abi = mag * jnp.sin(ai * dt)
    den = ar * ar + ai * ai
    nr = abr - 1.0
    cr = (nr * ar + abi * ai) / den
    ci = (abi * ar - nr * ai) / den
    bur = jnp.einsum('btgh,gph->btgp', uf, b_re.astype(f32))
    bui = jnp.einsum('btgh,gph->btgp', uf, b_im.astype(f32))
    xr, xi = _cmul(cr, ci, bur, bui)
    h0r, h0i = _cmul(abr, abi, h0_re.astype(f32), h0_im.astype(f32))
    xr = xr.at[:, 0].add(h0r)
    xi = xi.at[:, 0].add(h0i)
    a_r_t = jnp.broadcast_to(abr, xr.shape)
    a_i_t = jnp.broadcast_to(abi, xr.shape)
    _, _, hr, hi = lax.associative_scan(_ssm_combine, (a_r_t, a_i_t, xr, xi), axis=1)
    y = (jnp.einsum('btgp,ghp->btgh', hr, c_re.astype(f32))
         - jnp.einsum('btgp,ghp->btgh', hi, c_im.astype(f32))
         + d.astype(f32) * uf).reshape(bsz, t, S5_WIDTH)
    y = jax.nn.gelu(y)
    y = y * jax.nn.sigmoid(y @ w_glu.astype(f32) + b_glu.astype(f32))
    return y.astype(u.dtype), hr[:, -1].astype(u.dtype), hi[:, -1].astype(u.dtype)

def moba_attend(q, k_all, v_all, q_start):
    bsz, tq, nh, hd = q.shape
    tk = k_all.shape[1]
    nblk = -(-tk // MOBA_BLOCK)
    kpad = nblk * MOBA_BLOCK - tk

    def blocks(z):
        z = jnp.pad(z, ((0, 0), (0, kpad), (0, 0), (0, 0)))
        return z.reshape(bsz, nblk, MOBA_BLOCK, nh, hd).transpose(0, 3, 1, 2, 4)

    kb = blocks(k_all)
    vb = blocks(v_all)
    qc = min(MOBA_QCHUNK, tq)
    nq = -(-tq // qc)
    tqp = nq * qc
    qh = jnp.pad(q, ((0, 0), (0, tqp - tq), (0, 0), (0, 0))).transpose(0, 2, 1, 3).astype(jnp.float32)
    qpos = q_start + jnp.arange(tqp, dtype=jnp.int32)
    own = jnp.minimum(qpos // MOBA_BLOCK, nblk - 1)
    own_sel = jnp.broadcast_to(own[None, None, :, None], (bsz, nh, tqp, 1))
    n_past_sel = min(MOBA_TOPK, nblk - 1)
    if n_past_sel > 0:
        kmean = jnp.mean(kb.astype(jnp.float32), axis=3)
        gate = jnp.einsum('bhtd,bhnd->bhtn', qh, kmean)
        fully_past = jnp.arange(nblk)[None, :] < own[:, None]
        gate = jnp.where(fully_past[None, None], gate, NEG)
        top_val, top_idx = lax.top_k(gate, n_past_sel)
        sel = jnp.concatenate([top_idx.astype(jnp.int32), own_sel], axis=-1)
        valid = jnp.concatenate([top_val > 0.5 * NEG, jnp.ones_like(own_sel, dtype=bool)], axis=-1)
    else:
        sel = own_sel
        valid = jnp.ones_like(own_sel, dtype=bool)
    nsel = sel.shape[-1]

    def to_chunks(z):
        return jnp.moveaxis(z.reshape(bsz, nh, nq, qc, *z.shape[3:]), 2, 0)

    bi = jnp.arange(bsz)[:, None, None, None]
    hi = jnp.arange(nh)[None, :, None, None]
    offs = jnp.arange(MOBA_BLOCK, dtype=jnp.int32)
    scale = hd ** -0.5

    def attend_chunk(args):
        q_c, sel_c, val_c, pos_c = args
        kg = kb[bi, hi, sel_c].astype(jnp.float32)
        vg = vb[bi, hi, sel_c].astype(jnp.float32)
        logits = jnp.einsum('bhqd,bhqnkd->bhqnk', q_c, kg) * scale
        kpos = sel_c[..., None] * MOBA_BLOCK + offs
        mask = val_c[..., None] & (kpos <= pos_c[None, None, :, None, None])
        logits = jnp.where(mask, logits, NEG)
        w = jax.nn.softmax(logits.reshape(bsz, nh, qc, nsel * MOBA_BLOCK), axis=-1).reshape(logits.shape)
        return jnp.einsum('bhqnk,bhqnkd->bhqd', w, vg)

    out = lax.map(attend_chunk, (to_chunks(qh), to_chunks(sel), to_chunks(valid), qpos.reshape(nq, qc)))
    out = jnp.moveaxis(out, 0, 2).reshape(bsz, nh, tqp, hd)[:, :, :tq]
    return out.transpose(0, 2, 1, 3).astype(q.dtype)

def stick_breaking_attend(q, k_all, v_all, q_start):
    bsz, tq, nh, hd = q.shape
    scale = hd ** -0.5
    outs = []
    for s0 in range(0, tq, SB_QBLOCK):
        s1 = min(s0 + SB_QBLOCK, tq)
        kend = max(q_start + s1 - 1, 1)
        qb = q[:, s0:s1].astype(jnp.float32)
        kb = k_all[:, :kend].astype(jnp.float32)
        vb = v_all[:, :kend].astype(jnp.float32)
        z = jnp.einsum('bqhd,bkhd->bhqk', qb, kb) * scale
        tpos = q_start + jnp.arange(s0, s1)
        strict = jnp.arange(kend)[None, :] < tpos[:, None]
        log_beta = jnp.where(strict, jax.nn.log_sigmoid(z), NEG)
        log_keep = jnp.where(strict, jax.nn.log_sigmoid(-z), 0.0)
        later = lax.cumsum(log_keep, axis=3, reverse=True) - log_keep
        w = jnp.exp(log_beta + later)
        outs.append(jnp.einsum('bhqk,bkhd->bqhd', w, vb))
    return jnp.concatenate(outs, axis=1).astype(q.dtype)

def hgrn2(q, f_logit, v, g, lb, s0, g_norm):
    f32 = jnp.float32
    bsz, t, _ = q.shape
    f = lb + (1.0 - lb) * jax.nn.sigmoid(f_logit.astype(f32))
    log_f = jnp.log(f)
    k = 1.0 - f

    def heads(z):
        return z.astype(f32).reshape(bsz, t, HGRN_HEADS, HGRN_HEAD_DIM).transpose(0, 2, 1, 3)

    L = min(HGRN_CHUNK, t)
    nc = -(-t // L)
    pad = nc * L - t

    def chunks(z):
        z = jnp.pad(z, ((0, 0), (0, 0), (0, pad), (0, 0)))
        return jnp.moveaxis(z.reshape(bsz, HGRN_HEADS, nc, L, HGRN_HEAD_DIM), 2, 0)

    tri = jnp.tril(jnp.ones((L, L), dtype=bool))

    def step(S, xs):
        qc, kc, vc, lfc = xs
        b = jnp.cumsum(lfc, axis=2)
        diff = b[:, :, :, None, :] - b[:, :, None, :, :]
        decay = jnp.exp(jnp.where(tri[:, :, None], diff, NEG))
        att = jnp.einsum('bhtd,bhtsd,bhsd->bhts', qc, decay, kc)
        o = jnp.einsum('bhts,bhsv->bhtv', att, vc) + jnp.einsum('bhtd,bhdv->bhtv', qc * jnp.exp(b), S)
        bl = b[:, :, -1:, :]
        S = jnp.exp(bl[:, :, 0, :])[..., None] * S + jnp.einsum('bhsd,bhsv->bhdv', kc * jnp.exp(bl - b), vc)
        return S, o

    s_fin, o = lax.scan(step, s0.astype(f32), (chunks(heads(q)), chunks(heads(k)), chunks(heads(v)), chunks(heads(log_f))))
    o = jnp.moveaxis(o, 0, 2).reshape(bsz, HGRN_HEADS, nc * L, HGRN_HEAD_DIM)[:, :, :t].transpose(0, 2, 1, 3)
    o = o * lax.rsqrt(jnp.mean(o * o, axis=-1, keepdims=True) + EPS) * g_norm.astype(f32)
    o = o.reshape(bsz, t, HGRN_WIDTH) * jax.nn.silu(g.astype(f32))
    return o.astype(q.dtype), s_fin.astype(q.dtype)

def conv_ffn(a, buf, w_up, w_conv, b_conv, w_down):
    t = a.shape[1]
    u = a @ w_up
    full = jnp.concatenate([buf.astype(u.dtype), u], axis=1)
    c = b_conv
    for j in range(CONV_W):
        c = c + w_conv[j] * full[:, j:j + t]
    gate, val = jnp.split(c, 2, axis=-1)
    y = (jax.nn.gelu(gate) * val) @ w_down
    return y, full[:, t:]

def setup_inputs(seed: int = 0) -> dict:
    key = jax.random.key(seed)
    keys = jax.random.split(key, 48)
    counter = iter(range(48))
    f32 = jnp.float32

    def nrm(shape, scale=1.0):
        return scale * jax.random.normal(keys[next(counter)], shape, f32)

    def gain(shape):
        return 1.0 + nrm(shape, 0.1)

    n_pages = PAST_LEN // PAGE_SIZE
    n_used = DEC_BATCH * n_pages
    n_phys = (POOL_NUM * n_used + POOL_DEN - 1) // POOL_DEN
    inp = {}
    inp['x_prompt'] = nrm((BATCH, SEQ, D_MODEL))
    inp['x_sample'] = nrm((DEC_BATCH, DEC_SEQ, D_MODEL))
    inp['p_prompt'] = nrm((DEPTH, BATCH, SEQ, PLE_DIM))
    inp['p_sample'] = nrm((DEPTH, DEC_BATCH, DEC_SEQ, PLE_DIM))
    inp['cache_moba_k'] = nrm((N_A_LAYERS, n_phys, PAGE_SIZE, MOBA_HEADS, MOBA_HEAD_DIM))
    inp['cache_moba_v'] = nrm((N_A_LAYERS, n_phys, PAGE_SIZE, MOBA_HEADS, MOBA_HEAD_DIM))
    inp['state_s5_re'] = nrm((N_A_LAYERS, DEC_BATCH, S5_GROUPS, S5_STATE), 0.1)
    inp['state_s5_im'] = nrm((N_A_LAYERS, DEC_BATCH, S5_GROUPS, S5_STATE), 0.1)
    inp['state_hgrn'] = nrm((N_C_LAYERS, DEC_BATCH, HGRN_HEADS, HGRN_HEAD_DIM, HGRN_HEAD_DIM), 0.5)
    inp['cache_sb_k'] = nrm((N_C_LAYERS, n_phys, PAGE_SIZE, SB_HEADS, SB_HEAD_DIM))
    inp['cache_sb_v'] = nrm((N_C_LAYERS, n_phys, PAGE_SIZE, SB_HEADS, SB_HEAD_DIM))
    inp['state_ffn'] = nrm((DEPTH, DEC_BATCH, CONV_W - 1, 2 * D_FF))
    perm = jax.random.permutation(keys[next(counter)], n_phys)
    inp['page_table'] = perm[:n_used].reshape(DEC_BATCH, n_pages).astype(jnp.int32)
    inp['g_mix_pre'] = gain((DEPTH, D_MODEL))
    inp['g_mix_post'] = gain((DEPTH, D_MODEL))
    inp['g_ffn_pre'] = gain((DEPTH, D_MODEL))
    inp['g_ffn_post'] = gain((DEPTH, D_MODEL))
    inp['w_ffn_up'] = nrm((DEPTH, D_MODEL, 2 * D_FF), D_MODEL ** -0.5)
    inp['w_ffn_conv'] = nrm((DEPTH, CONV_W, 2 * D_FF), CONV_W ** -0.5)
    inp['b_ffn_conv'] = nrm((DEPTH, 2 * D_FF), 0.02)
    inp['w_ffn_down'] = nrm((DEPTH, D_FF, D_MODEL), D_FF ** -0.5)
    inp['w_ple_proj'] = nrm((DEPTH, PLE_DIM, D_MODEL), PLE_DIM ** -0.5)
    inp['w_ple_gate'] = nrm((DEPTH, D_MODEL, D_MODEL), D_MODEL ** -0.5)
    inp['g_ple'] = gain((DEPTH, D_MODEL))
    inp['w_in_a'] = nrm((N_A_LAYERS, D_MODEL, IN_A), D_MODEL ** -0.5)
    inp['w_out_a'] = nrm((N_A_LAYERS, MIX_WIDTH, D_MODEL), MIX_WIDTH ** -0.5)
    inp['s5_a_re'] = -0.5 + nrm((N_A_LAYERS, S5_GROUPS, S5_STATE), 0.01)
    inp['s5_a_im'] = jnp.pi * jnp.arange(S5_STATE, dtype=f32) + nrm((N_A_LAYERS, S5_GROUPS, S5_STATE), 0.01)
    inp['s5_log_dt'] = jax.random.uniform(keys[next(counter)], (N_A_LAYERS, S5_GROUPS), f32,
                                          minval=math.log(S5_DT_MIN), maxval=math.log(S5_DT_MAX))
    inp['s5_b_re'] = nrm((N_A_LAYERS, S5_GROUPS, S5_STATE, S5_GROUP), (2 * S5_GROUP) ** -0.5)
    inp['s5_b_im'] = nrm((N_A_LAYERS, S5_GROUPS, S5_STATE, S5_GROUP), (2 * S5_GROUP) ** -0.5)
    inp['s5_c_re'] = nrm((N_A_LAYERS, S5_GROUPS, S5_GROUP, S5_STATE), (2 * S5_STATE) ** -0.5)
    inp['s5_c_im'] = nrm((N_A_LAYERS, S5_GROUPS, S5_GROUP, S5_STATE), (2 * S5_STATE) ** -0.5)
    inp['s5_d'] = nrm((N_A_LAYERS, S5_GROUPS, S5_GROUP))
    inp['s5_w_glu'] = nrm((N_A_LAYERS, S5_WIDTH, S5_WIDTH), S5_WIDTH ** -0.5)
    inp['s5_b_glu'] = nrm((N_A_LAYERS, S5_WIDTH), 0.02)
    inp['w_in_c'] = nrm((N_C_LAYERS, D_MODEL, IN_C), D_MODEL ** -0.5)
    inp['w_out_c'] = nrm((N_C_LAYERS, MIX_WIDTH, D_MODEL), MIX_WIDTH ** -0.5)
    inp['hgrn_lb'] = nrm((DEPTH, HGRN_WIDTH))
    inp['g_hgrn_norm'] = gain((N_C_LAYERS, HGRN_HEAD_DIM))
    return inp

def reference(x_prompt, x_sample, p_prompt, p_sample, cache_moba_k, cache_moba_v, state_s5_re, state_s5_im,
              state_hgrn, cache_sb_k, cache_sb_v, state_ffn, page_table,
              g_mix_pre, g_mix_post, g_ffn_pre, g_ffn_post, w_ffn_up, w_ffn_conv, b_ffn_conv, w_ffn_down,
              w_ple_proj, w_ple_gate, g_ple,
              w_in_a, w_out_a, s5_a_re, s5_a_im, s5_log_dt, s5_b_re, s5_b_im, s5_c_re, s5_c_im, s5_d,
              s5_w_glu, s5_b_glu,
              w_in_c, w_out_c, hgrn_lb, g_hgrn_norm):
    f32 = jnp.float32
    n_pages = page_table.shape[1]
    past_len = n_pages * cache_moba_k.shape[2]
    lb_soft = jax.nn.softmax(hgrn_lb.astype(f32), axis=0)
    lower_bounds = jnp.cumsum(lb_soft, axis=0) - lb_soft[0:1]
    mw = MOBA_HEADS * MOBA_HEAD_DIM
    sw = SB_HEADS * SB_HEAD_DIM

    def paged_rows(pool, j):
        rows = pool[j, page_table]
        return rows.reshape(rows.shape[0], past_len, rows.shape[3], rows.shape[4])

    def run(x, p, q_start, s5_re0, s5_im0, hgrn0, ffn0, has_past):
        bsz, t, _ = x.shape
        pos = q_start + jnp.arange(t, dtype=jnp.int32)
        h = x
        mk, mv, sr, si, hs, sk, sv, fb = [], [], [], [], [], [], [], []
        for i in range(DEPTH):
            j = i // 2
            a = rmsnorm(h, g_mix_pre[i])
            if i % 2 == 0:
                z = a @ w_in_a[j]
                u = z[..., :S5_WIDTH]
                qkv = z[..., S5_WIDTH:].reshape(bsz, t, 3, MOBA_HEADS, MOBA_HEAD_DIM)
                qm = partial_rope(qkv[:, :, 0], pos)
                km = partial_rope(qkv[:, :, 1], pos)
                vm = qkv[:, :, 2]
                y_s5, hr, hi = s5_mixer(u, s5_re0[j], s5_im0[j], s5_a_re[j], s5_a_im[j], s5_log_dt[j],
                                        s5_b_re[j], s5_b_im[j], s5_c_re[j], s5_c_im[j], s5_d[j],
                                        s5_w_glu[j], s5_b_glu[j])
                if has_past:
                    k_all = jnp.concatenate([paged_rows(cache_moba_k, j).astype(km.dtype), km], axis=1)
                    v_all = jnp.concatenate([paged_rows(cache_moba_v, j).astype(vm.dtype), vm], axis=1)
                else:
                    k_all, v_all = km, vm
                y_mb = moba_attend(qm, k_all, v_all, q_start)
                mix = jnp.concatenate([y_s5, y_mb.reshape(bsz, t, mw)], axis=-1) @ w_out_a[j]
                mk.append(km)
                mv.append(vm)
                sr.append(hr)
                si.append(hi)
            else:
                z = a @ w_in_c[j]
                q_h = z[..., 0:HGRN_WIDTH]
                f_h = z[..., HGRN_WIDTH:2 * HGRN_WIDTH]
                i_h = z[..., 2 * HGRN_WIDTH:3 * HGRN_WIDTH]
                g_h = z[..., 3 * HGRN_WIDTH:4 * HGRN_WIDTH]
                qkv = z[..., 4 * HGRN_WIDTH:].reshape(bsz, t, 3, SB_HEADS, SB_HEAD_DIM)
                qd = qkv[:, :, 0]
                kd = qkv[:, :, 1]
                vd = qkv[:, :, 2]
                y_hg, s_fin = hgrn2(q_h, f_h, i_h, g_h, lower_bounds[i], hgrn0[j], g_hgrn_norm[j])
                if has_past:
                    k_all = jnp.concatenate([paged_rows(cache_sb_k, j).astype(kd.dtype), kd], axis=1)
                    v_all = jnp.concatenate([paged_rows(cache_sb_v, j).astype(vd.dtype), vd], axis=1)
                else:
                    k_all, v_all = kd, vd
                y_sb = stick_breaking_attend(qd, k_all, v_all, q_start)
                mix = jnp.concatenate([y_hg, y_sb.reshape(bsz, t, sw)], axis=-1) @ w_out_c[j]
                hs.append(s_fin)
                sk.append(kd)
                sv.append(vd)
            h = h + rmsnorm(mix, g_mix_post[i])
            f, buf = conv_ffn(rmsnorm(h, g_ffn_pre[i]), ffn0[i], w_ffn_up[i], w_ffn_conv[i], b_ffn_conv[i], w_ffn_down[i])
            h = h + rmsnorm(f, g_ffn_post[i])
            fb.append(buf)
            ple = (p[i] @ w_ple_proj[i]) * jax.nn.sigmoid(h @ w_ple_gate[i])
            h = h + rmsnorm(ple, g_ple[i])
        return (h, jnp.stack(mk), jnp.stack(mv), jnp.stack(sr), jnp.stack(si), jnp.stack(hs),
                jnp.stack(sk), jnp.stack(sv), jnp.stack(fb))

    bp = x_prompt.shape[0]
    dt = x_prompt.dtype
    (y_prompt, moba_k_prompt, moba_v_prompt, s5_re_prompt, s5_im_prompt, hgrn_prompt,
     sb_k_prompt, sb_v_prompt, ffn_prompt) = run(
        x_prompt, p_prompt, 0,
        jnp.zeros((N_A_LAYERS, bp, S5_GROUPS, S5_STATE), dt),
        jnp.zeros((N_A_LAYERS, bp, S5_GROUPS, S5_STATE), dt),
        jnp.zeros((N_C_LAYERS, bp, HGRN_HEADS, HGRN_HEAD_DIM, HGRN_HEAD_DIM), dt),
        jnp.zeros((DEPTH, bp, CONV_W - 1, 2 * D_FF), dt),
        False)
    (y_sample, moba_k_sample, moba_v_sample, s5_re_sample, s5_im_sample, hgrn_sample,
     sb_k_sample, sb_v_sample, ffn_sample) = run(
        x_sample, p_sample, past_len, state_s5_re, state_s5_im, state_hgrn, state_ffn, True)
    return (y_prompt, y_sample,
            moba_k_prompt, moba_v_prompt, s5_re_prompt, s5_im_prompt, hgrn_prompt, sb_k_prompt, sb_v_prompt, ffn_prompt,
            moba_k_sample, moba_v_sample, s5_re_sample, s5_im_sample, hgrn_sample, sb_k_sample, sb_v_sample, ffn_sample)


_drawn_inputs = setup_inputs


def setup_inputs(seed=0):
    import zlib

    import numpy as np

    out = dict(_drawn_inputs(seed))
    spreads = {}
    factors = {'b_ffn_conv': 2.694, 's5_a_re': 4.078, 's5_b_glu': 6.896}
    for name, (base, spread) in spreads.items():
        noise = np.random.default_rng([zlib.crc32(name.encode()), seed]).standard_normal(out[name].shape)
        drawn = base * np.exp(spread * noise) if base else spread * noise
        out[name] = jnp.asarray(drawn.astype(out[name].dtype))
    for name, factor in factors.items():
        out[name] = (out[name] * factor).astype(out[name].dtype)
    return out
```

```python
from contextlib import ExitStack

import concourse.bass as bass
import numpy as np
from concourse import mybir

F32 = mybir.dt.float32
F32R = mybir.dt.float32r
I32 = mybir.dt.int32
ALU = mybir.AluOpType
ACT = mybir.ActivationFunctionType
AXX = mybir.AxisListType.X

P = 128
D = 1024
KD = D // P
TP = 512
NB = 8
TS = 8
NS = NB * TS
T = TP + NS
HALF = T // 2
DEPTH = 2
DFF = 2816
FT = DFF // P
PLE = 256
PAST = 1024
PAGE = 128
NPG = PAST // PAGE
NH = 8
HD = 64
GRP = 32
SC = 16
SP_ = 64
GP = GRP // 2
CH = 8
NC_P = TP // CH
NCH = T // CH
HH = 4
CL = 128
NCL = TP // CL
LEVELS = [64, 32, 16, 8, 4, 2, 1]
EPS = 1e-6
NEG = -1e30
ATT_SCALE = HD ** -0.5
RING = 8
SLAB = KD * P
DSLAB = 11 * P
ARENA = 26300
DRING = 3
RAW = 4
AHEAD = 3

VEC = {}
_at = 0
for _name, _n in (("g_mix_pre", KD), ("g_mix_post", KD), ("g_ffn_pre", KD), ("g_ffn_post", KD), ("g_ple", KD),
                  ("conv0", 2 * FT), ("conv1", 2 * FT), ("conv2", 2 * FT), ("conv_b", 2 * FT),
                  ("b_glu", 4), ("lb0", 4), ("lb1", 4), ("g_hgrn", 1)):
    VEC[_name] = _at
    _at += _n
NVEC = _at

CON = {"ident": 0, "ones": P, "rot": 2 * P, "tri": 3 * P}
NCON = 4 * P + NB
LCON = [{"cos": 0, "sin": T, "causal": 2 * T, "new": 2 * T + P},
        {"reset": 0, "level": T, "causal": T + 7 * 64, "new": T + 7 * 64 + P}]
NLCON = 2 * T + P + NB // 2 * NS


def build(nc, A):
    with ExitStack() as ctx:
        def sb(name, cols, dt=F32, parts=P):
            return ctx.enter_context(nc.sbuf_tensor("sb_" + name, [parts, cols], dt))

        def sem(name):
            return ctx.enter_context(nc.semaphore(name))

        rounded = {}

        def sb2(name, cols):
            with nc.sbuf_tensor("sb_" + name + "_r", [P, cols], F32R) as r:
                pass
            x = sb(name, cols)
            rounded[x[:, :].tensor.name] = r[:, :].tensor
            return x

        def fr(x):
            return bass.AP(tensor=rounded[x.tensor.name], offset=x.offset, ap=x.ap)

        ring = sb2("ring", RING * SLAB)
        h_sb = sb("h_sb", KD * T)
        a_sb = sb2("a_sb", KD * T)
        y_sb = sb2("y_sb", KD * T)
        con = sb("con", NCON)
        lcon = sb("lcon", NLCON)
        vec = sb("vec", DEPTH * NVEC)
        small = sb("small", 64)
        rstd = sb("rstd", T)
        pages = sb("pages", NB * NPG, I32, 1)
        arena = sb2("arena", ARENA)
        psum = ctx.enter_context(nc.psum_tensor("psum", [P, 8, 512], F32))

        h = h_sb[:, :].rearrange("p (k t) -> p k t", k=KD)
        a = a_sb[:, :].rearrange("p (k t) -> p k t", k=KD)
        y = y_sb[:, :].rearrange("p (k t) -> p k t", k=KD)
        wx = arena[:, ARENA - 4 * SLAB:ARENA].rearrange("p (s k n) -> p s k n", s=4, k=KD)
        slabs = ring[:, :].rearrange("p (s k n) -> p s k n", s=RING, k=KD)
        dslabs = ring[:, 0:DRING * DSLAB].rearrange("p (s k n) -> p s k n", s=DRING, k=11)
        split = [(z[:, at + 2 * i], z[:, at + 1 + 2 * i]) for z, at in ((slabs, RAW), (wx, 0)) for i in range(2)]
        dsplit = [[z[:, at + i * DSLAB:at + (i + 1) * DSLAB].rearrange("p (k n) -> p k n", k=11) for i in range(2)]
                  for z, at in ((ring, DRING * DSLAB), (y_sb, 0))]
        ident, ones, rot, tri = (con[:, CON[x]:CON[x] + P] for x in ("ident", "ones", "rot", "tri"))
        eps_col = small[:, 0:1]
        one_col = small[:, 1:2]

        def pair(s, parts=P):
            return psum[0:parts, 2 * s:2 * s + 2, 0:HALF]

        def halves(x):
            return x.rearrange("p (a n) -> p a n", a=2)

        def cut(at, n):
            return arena[:, at:at + n]

        def vcol(layer, name, k=0):
            c = layer * NVEC + VEC[name] + k
            return vec[:, c:c + 1]

        pe_stage, act_stage, dve_stage = sem("pe_stage"), sem("act_stage"), sem("dve_stage")
        x_in = [sem(f"x_in{k}") for k in range(KD)]
        con_in, vec_in, lcon_in, pages_in = (sem(x) for x in ("con_in", "vec_in", "lcon_in", "pages_in"))
        slab_in = [sem(f"slab_in{i}") for i in range(RING)]
        acc_ready = sem("acc_ready")
        raw_in = [sem(f"raw_in{i}") for i in range(RAW)]
        draw_in = [sem(f"draw_in{i}") for i in range(DRING)]
        wh_ready, wl_ready, xh_ready, xl_ready, part_done, h_new = (
            sem(x) for x in ("wh_ready", "wl_ready", "xh_ready", "xl_ready", "part_done", "h_new"))
        dve_step, act_step = sem("dve_step"), sem("act_step")
        sq_ready, rs_ready = sem("sq_ready"), sem("rs_ready")
        stored = sem("stored")

        class Steps:

            def __init__(self, eng, s):
                self.eng, self.s, self.base, self.n = eng, s, 0, 0

            def do(self, ins):
                self.n += 1
                ins.then_inc(self.s, 1)
                self.eng.wait_ge(self.s, self.base + self.n)

            def enter(self, i, per):
                self.outer, self.per = self.base + self.n, per
                self.base, self.n = self.outer + i * per, 0

            def leave(self, rounds):
                assert self.n == self.per, self.n
                self.base, self.n = self.outer + rounds * self.per, 0

        class Engine:

            def __init__(self, eng, own, step=None):
                self.eng, self.own = eng, own
                self.stage, self.norms, self.ups, self.layer, self.pre = 0, 0, 0, 1, 0
                self.fills = [0] * RING
                self.raws, self.splits, self.parts, self.downs, self.adds = [0] * RAW, 0, 0, 0, 0
                self.st = Steps(eng, step) if step is not None else None

            def fence(self):
                self.eng.drain().then_inc(self.own, 1)
                self.stage += 1
                for s in (pe_stage, act_stage, dve_stage):
                    self.eng.wait_ge(s, self.stage)

        block = ctx.enter_context(nc.Block())

        _c = [0]

        def take(n):
            _c[0] += n
            return _c[0] - n

        zq_at = take(8 * T)
        zqk = cut(zq_at, 8 * T).rearrange("p (m t) -> p m t", m=8)
        vt = cut(take(4 * 512), 4 * 512).rearrange("p (i n) -> p i n", i=4)
        vs = cut(take(512), 512)
        mixer_free = _c[0]
        uT_flat = cut(take(GRP * NCH), GRP * NCH)
        uT = uT_flat.rearrange("p (g c) -> p g c", g=GRP)
        NQ = GP * (CH + 1) * SC
        q5 = [cut(take(NQ), NQ).rearrange("p (g s c) -> p g s c", g=GP, s=CH + 1) for _ in range(2)]
        mt_at = take(GRP * P)
        mt = cut(mt_at, GRP * P).rearrange("p (g n) -> p g n", g=GRP)
        xwt = [cut(mt_at + i * 2048, 2048).rearrange("p (g s c) -> p g s c", g=GP, s=CH) for i in range(2)]
        piece_at = [take(1024), take(1024)]
        piece = [cut(z, 1024).rearrange("p (s n) -> p s n", s=CH) for z in piece_at]
        upiece = [cut(z, 1024).rearrange("p (g n) -> p g n", g=8) for z in piece_at]
        hin_flat = cut(take(2 * GP * NCH), 2 * GP * NCH)
        hin = [hin_flat[:, i * GP * NCH:(i + 1) * GP * NCH].rearrange("p (g c) -> p g c", g=GP) for i in range(2)]
        par_at = take(3 * GP)
        ar, ai, ldt = (cut(par_at + i * GP, GP) for i in range(3))
        bc_at = take(4 * GP * SC)
        b_re, b_im, c_re, c_im = (cut(bc_at + i * 256, 256).rearrange("p (g c) -> p g c", g=GP) for i in range(4))
        d_at = take(GRP)
        d16 = arena[0:SC, d_at:d_at + GRP]
        st_at = take(2 * GP * NB)
        st0 = [cut(st_at + i * 128, 128).rearrange("p (g b) -> p g b", g=GP) for i in range(2)]
        so_at = take(2 * GP * 9)
        s5o = [cut(so_at + i * 144, 144).rearrange("p (g b) -> p g b", g=GP) for i in range(2)]
        bp = [cut(take(256), 256).rearrange("p (g c) -> p g c", g=GP) for _ in range(2)]
        powr = [cut(take(144), 144).rearrange("p (g s) -> p g s", g=GP) for _ in range(2)]
        tiny_at = take(26 * GP)
        tiny = [cut(tiny_at + i * GP, GP) for i in range(20)]
        assert _c[0] <= ARENA, _c[0]
        xw = [y_sb[:, i * 2048:(i + 1) * 2048].rearrange("p (g n) -> p g n", g=GP) for i in range(2)]
        kp = [y_sb[0:SC, i * 1024:(i + 1) * 1024].rearrange("p (g n) -> p g n", g=8) for i in range(2)]
        tmp5 = [y_sb[:, 2048 + i * 1024:2048 + (i + 1) * 1024].rearrange("p (g c) -> p g c", g=GP) for i in range(2)]
        ph = [a_sb[:, i * 1024:(i + 1) * 1024].rearrange("p (g c) -> p g c", g=GP) for i in range(2)]
        gst = [a_sb[:, 2048 + i * 1024:2048 + (i + 1) * 1024].rearrange("p (g c) -> p g c", g=GP) for i in range(2)]

        copied = {"act": sem("act_copied"), "dve": sem("dve_copied")}

        class Tile:

            def __init__(self, s, n, out, held):
                self.s, self.n, self.out, self.held = s, n, out, held

        class Acc:

            def __init__(self):
                self.n = 0
                self.count = {"act": 0, "dve": 0}
                self.last = [None] * 4

            def next(self, by="act"):
                s, held = self.n % 4, self.last[self.n % 4]
                self.n += 1
                self.count[by] += 1
                self.last[s] = (copied[by], self.count[by])
                return Tile(s, self.n, self.last[s], held)

            def skip(self, count, by="act"):
                for _ in range(count):
                    self.next(by)

        def wait_emptied(e, t):
            if t.held is not None:
                e.eng.wait_ge(*t.held)

        def wait_filled(e, t):
            e.eng.wait_ge(acc_ready, t.n)

        def wait_slab(e, slot):
            e.fills[slot] += 1
            e.eng.wait_ge(slab_in[slot], 16 * e.fills[slot])

        class Loader:

            def __init__(self, sp):
                self.sp, self.row, self.drow, self.splits = sp, 0, 0, 0
                self.until = [None] * (RING * KD)

            def load(self, slot, used_by):
                self.free(slot * KD, KD, (acc_ready, used_by))
                self.sp.dma_start(slabs[:, slot], A["w8"][self.row].rearrange("p (k n) -> p k n", k=KD))\
                    .then_inc(slab_in[slot], 16)
                self.row += 1

            def load_raw(self):
                slot = self.raw_at % RAW
                self.raw_at += 1
                self.splits += 1
                self.free(slot * KD, KD, (wl_ready, self.splits))
                self.sp.dma_start(slabs[:, slot], A["w8"][self.row].rearrange("p (k n) -> p k n", k=KD))\
                    .then_inc(raw_in[slot], 16)
                self.row += 1

            def begin_split(self):
                self.raw_at = 0

            def end_split(self, at):
                self.until[RAW * KD:] = [(acc_ready, at)] * (KD * (RING - RAW))

            def load_down(self, n):
                slot = n % DRING
                self.splits += 1
                self.free(slot * 11, 11, (wl_ready, self.splits))
                self.sp.dma_start(dslabs[:, slot], A["wd"][self.drow].rearrange("p (k n) -> p k n", k=11))\
                    .then_inc(draw_in[slot], 16)
                self.drow += 1

            def free(self, at, n, then):
                held = [u for u in self.until[at:at + n] if u is not None]
                for s in (acc_ready, wl_ready):
                    need = [v for t, v in held if t is s]
                    if need:
                        self.sp.wait_ge(s, max(need))
                self.until[at:at + n] = [then] * n

        def act_high(e, src, dst, ready):
            e.eng.activation(fr(dst), src, ACT.Copy).then_inc(ready, 1)

        def dve_low(e, src, high, dst, ready):
            e.eng.tensor_tensor(fr(dst), src, fr(high).bitcast(F32), ALU.subtract).then_inc(ready, 1)

        def act_split_rhs(e, src, high, after=None):
            for k in range(len(src)):
                if after is not None:
                    e.eng.wait_ge(after[0], after[1] + k + 1)
                act_high(e, src[k], high[k], xh_ready)
            e.parts += len(src)

        def dve_split_rhs(e, src, high, low):
            for k in range(len(src)):
                e.eng.wait_ge(xh_ready, e.parts + k + 1)
                dve_low(e, src[k], high[k], low[k], xl_ready)
            e.parts += len(src)

        def tiles_of(x, n=KD):
            return [x[:, k, :] for k in range(n)]

        def act_split_slab(e, n, used, off=0):
            e.raws[n % RAW] += 1
            e.eng.wait_ge(raw_in[n % RAW], 16 * e.raws[n % RAW])
            if used is not None:
                e.eng.wait_ge(acc_ready, used)
            act_high(e, slabs[:, n % RAW], split[(n + off) % 4][0], wh_ready)

        def dve_split_slab(e, n, off=0):
            e.splits += 1
            e.eng.wait_ge(wh_ready, e.splits)
            dve_low(e, slabs[:, n % RAW], *split[(n + off) % 4], wl_ready)

        def mm_split(e, out, w, x, kb, first=True, last=True, x_parts=None):
            for k in range(kb):
                if x_parts is not None:
                    e.eng.wait_ge(xl_ready, x_parts + k + 1)
                for half in range(2):
                    cols = slice(half * HALF, (half + 1) * HALF)
                    for i, (p, q) in enumerate(((0, 0), (0, 1), (1, 0))):
                        ins = e.eng.matmul(out[:, half, :], fr(w[p][:, k, :]), fr(x[q][:, k, cols]),
                                           start=(first and k == 0 and i == 0), stop=(last and k == kb - 1 and i == 2))
            return ins

        def mm_tile(e, out, w, rhs, kb, first=True, last=True):
            for half in range(2):
                for k in range(kb):
                    ins = e.eng.matmul(out[:, half, :], w[:, k, :], rhs[:, k, half * HALF:(half + 1) * HALF],
                                       start=(first and k == 0), stop=(last and k == kb - 1))
            return ins

        def pe_norm(e, acc, sq):
            t = acc.next("act")
            wait_emptied(e, t)
            for k in range(KD):
                e.eng.wait_ge(sq_ready, KD * e.norms + k + 1)
                for half in range(2):
                    last = e.eng.matmul(pair(t.s)[:, half, :], ones, sq[:, k, half * HALF:(half + 1) * HALF],
                                        start=(k == 0), stop=(k == KD - 1))
            last.then_inc(acc_ready, 1)
            e.norms += 1

        def act_norm(e, acc, src, sq, fresh=False, arrive=None):
            e.eng.preload_act_table_set("natural_log_exp_and_others")
            for k in range(KD):
                if arrive is not None:
                    e.eng.wait_ge(arrive[k], 16)
                if fresh:
                    e.eng.wait_ge(h_new, e.adds + k + 1)
                e.eng.activation(sq[:, k, :], src[:, k, :], ACT.Square).then_inc(sq_ready, 1)
            if fresh:
                e.adds += KD
            t = acc.next("act")
            wait_filled(e, t)
            e.eng.activation(halves(rstd[:, :]), pair(t.s), ACT.Ln, scale=1.0 / D, bias=eps_col)\
                .then_inc(copied["act"], 1)
            e.eng.wait_ge(*t.out)
            e.eng.activation(rstd[:, :], rstd[:, :], ACT.Exp, scale=-0.5).then_inc(rs_ready, 1)

        def dve_norm(e, acc, src, dst, layer, gain, residual=False, ready=None):
            acc.next("act")
            e.norms += 1
            e.eng.wait_ge(rs_ready, e.norms)
            for k in range(KD):
                last = e.eng.scalar_tensor_tensor(dst[:, k, :], src[:, k, :], vcol(layer, gain, k), rstd[:, :],
                                                  ALU.mult, ALU.mult)
                if residual:
                    e.st.do(last)
                    e.eng.tensor_tensor(h[:, k, :], h[:, k, :], dst[:, k, :], ALU.add).then_inc(h_new, 1)
                elif ready is not None:
                    last.then_inc(ready, 1)

        def cmul(e, out, x, z, t, conj=False, negate_im=False):
            tt = e.eng.tensor_tensor
            e.st.do(tt(t[0], x[0], z[0], ALU.mult))
            e.st.do(tt(t[1], x[1], z[1], ALU.mult))
            e.st.do(tt(t[0], t[0], t[1], ALU.add if conj else ALU.subtract))
            e.st.do(tt(t[1], x[1], z[0], ALU.mult))
            e.st.do(tt(out[1], x[0], z[1], ALU.mult))
            if negate_im:
                e.st.do(e.eng.scalar_tensor_tensor(out[1], out[1], -1.0, t[1], ALU.mult, ALU.subtract))
            else:
                e.st.do(tt(out[1], t[1], out[1], ALU.subtract if conj else ALU.add))
            e.st.do(e.eng.tensor_copy(out[0], t[0]))

        s5_in = sem("s5_in")
        (dt, adt, mag, mag8, kf, r, r2, sn, cs, nr, den, rden, crr, cii, u0, u1) = tiny[:16]
        TWO_PI = 2 * np.pi
        MAGIC = 1.5 * 2.0 ** 23

        def dve_exp(e, dst, x, kf, r, u0):
            v, do = e.eng, e.st.do
            hi = 0.693359375
            do(v.tensor_scalar(kf, x, float(1 / np.log(2)), -126.0, ALU.mult, ALU.max))
            do(v.tensor_scalar(kf, kf, 127.0, MAGIC, ALU.min, ALU.add))
            do(v.tensor_scalar(kf, kf, MAGIC, None, ALU.subtract))
            do(v.scalar_tensor_tensor(r, kf, -hi, x, ALU.mult, ALU.add))
            do(v.scalar_tensor_tensor(r, kf, float(hi - np.log(2)), r, ALU.mult, ALU.add))
            do(v.tensor_scalar(r, r, -1.0, 1.0, ALU.max, ALU.min))
            do(v.tensor_scalar(u0, r, 1.0 / 5040, None, ALU.mult))
            for c in (720, 120, 24, 6, 2, 1):
                do(v.scalar_tensor_tensor(u0, u0, 1.0 / c, r, ALU.add, ALU.mult))
            do(v.tensor_scalar(kf, kf, 127.0, 2.0 ** 23, ALU.add, ALU.mult))
            do(v.tensor_copy(r.bitcast(I32), kf))
            do(v.scalar_tensor_tensor(dst, u0, 1.0, r, ALU.add, ALU.mult))

        def dve_s5_params(e):
            v, do = e.eng, e.st.do
            v.wait_ge(s5_in, 16 * len(S5_LOADS))
            dve_exp(e, dt, ldt, kf, r, u0)
            do(v.tensor_tensor(adt, ar, dt, ALU.mult))
            dve_exp(e, mag, adt, kf, r, u0)
            do(v.tensor_tensor(mag8, mag, mag, ALU.mult))
            do(v.tensor_tensor(mag8, mag8, mag8, ALU.mult))
            do(v.tensor_tensor(mag8, mag8, mag8, ALU.mult))
            do(v.tensor_tensor(adt, ai, dt, ALU.mult))
            do(v.tensor_scalar(kf, adt, 1.0 / TWO_PI, MAGIC, ALU.mult, ALU.add))
            do(v.tensor_scalar(kf, kf, MAGIC, None, ALU.subtract))
            c1 = 6.28125
            c2 = float(np.float32(TWO_PI - c1))
            do(v.scalar_tensor_tensor(r, kf, -c1, adt, ALU.mult, ALU.add))
            do(v.scalar_tensor_tensor(r, kf, -c2, r, ALU.mult, ALU.add))
            do(v.scalar_tensor_tensor(r, kf, -float(TWO_PI - c1 - c2), r, ALU.mult, ALU.add))
            do(v.tensor_scalar(r, r, 0.25, None, ALU.mult))
            do(v.tensor_tensor(r2, r, r, ALU.mult))
            do(v.tensor_scalar(sn, r2, 1.0 / 362880, None, ALU.mult))
            for c in (-5040, 120, -6):
                do(v.scalar_tensor_tensor(sn, sn, 1.0 / c, r2, ALU.add, ALU.mult))
            do(v.scalar_tensor_tensor(sn, sn, 1.0, r, ALU.add, ALU.mult))
            do(v.tensor_scalar(cs, r2, -1.0 / 3628800, None, ALU.mult))
            for c in (40320, -720, 24, -2):
                do(v.scalar_tensor_tensor(cs, cs, 1.0 / c, r2, ALU.add, ALU.mult))
            do(v.tensor_scalar(cs, cs, 1.0, None, ALU.add))
            for _ in range(2):
                do(v.tensor_tensor(u0, sn, sn, ALU.mult))
                do(v.scalar_tensor_tensor(sn, sn, 2.0, cs, ALU.mult, ALU.mult))
                do(v.tensor_scalar(cs, u0, -2.0, 1.0, ALU.mult, ALU.add))

        tq5 = [y_sb[:, 0:NQ], y_sb[:, NQ:2 * NQ]]

        def dve_s5_tables(e):
            v, do = e.eng, e.st.do
            tt, ts = v.tensor_tensor, v.tensor_scalar
            pr, pi = powr
            do(v.memset(pr[:, :, 0:1], 1.0))
            do(v.memset(pi[:, :, 0:1], 0.0))
            do(tt(pr[:, :, 1], mag, cs, ALU.mult))
            do(tt(pi[:, :, 1], mag, sn, ALU.mult))
            do(ts(nr, pr[:, :, 1], -1.0, None, ALU.add))
            do(tt(den, ar, ar, ALU.mult))
            do(tt(u0, ai, ai, ALU.mult))
            do(tt(den, den, u0, ALU.add))
            do(v.reciprocal(rden, den))
            do(tt(u0, nr, ar, ALU.mult))
            do(tt(u1, pi[:, :, 1], ai, ALU.mult))
            do(tt(u0, u0, u1, ALU.add))
            do(tt(crr, u0, rden, ALU.mult))
            do(tt(u0, pi[:, :, 1], ar, ALU.mult))
            do(tt(u1, nr, ai, ALU.mult))
            do(tt(u0, u0, u1, ALU.subtract))
            do(tt(cii, u0, rden, ALU.mult))

            def wide(x, n):
                return x.unsqueeze(2).to_broadcast([P, GP, n])

            def temps(n):
                return [z[:, 0:GP * n].rearrange("p (g c) -> p g c", g=GP) for z in tq5]

            cmul(e, bp, (b_re, b_im), (wide(crr, SC), wide(cii, SC)), temps(SC))
            for n in (1, 2, 4):
                cmul(e, [z[:, :, n + 1:2 * n + 1] for z in powr], [z[:, :, 1:n + 1] for z in powr],
                     [z[:, :, n:n + 1].to_broadcast([P, GP, n]) for z in powr], temps(n))

            def over_steps(z, n):
                return z.unsqueeze(2).to_broadcast([P, GP, n, SC])

            def over_channels(z, n):
                return z.unsqueeze(3).to_broadcast([P, GP, n, SC])

            def temps4(n):
                return [z[:, 0:GP * n * SC].rearrange("p (g s c) -> p g s c", g=GP, s=n) for z in tq5]

            cmul(e, q5, [over_steps(z, CH + 1) for z in (c_re, c_im)], [over_channels(z, CH + 1) for z in powr],
                 temps4(CH + 1), negate_im=True)
            cmul(e, xwt, [over_steps(z, CH) for z in bp], [over_channels(z[:, :, CH - 1::-1], CH) for z in powr],
                 temps4(CH))

        def pe_proj_a(e, acc):
            pe = e.eng
            piece_copied = [None] * 4
            for j in range(5):
                if j < 4:
                    wait_slab(e, j)
                    t = acc.next("act")
                    wait_emptied(e, t)
                    for st in range(CH):
                        for k in range(KD):
                            last = pe.matmul(psum[0:NCH, 2 * t.s + st // 4, (st % 4) * P:(st % 4 + 1) * P],
                                             a[:, k, st::CH], slabs[:, j, k, :], start=(k == 0), stop=(k == KD - 1))
                    last.then_inc(acc_ready, 1)
                    piece_copied[j] = t.out
                if j >= 1:
                    pe.wait_ge(*piece_copied[j - 1])
                    t = acc.next("act")
                    wait_emptied(e, t)
                    for g in range(8):
                        last = pe.transpose(psum[:, 2 * t.s + g // 4, (g % 4) * NCH:(g % 4 + 1) * NCH],
                                            upiece[(j - 1) % 2][0:NCH, g, :], ident[0:NCH, 0:NCH])
                    last.then_inc(acc_ready, 1)
            pe_value_rows(e, acc, 4, a)
            pe_rope(e, acc)

        def pe_rope(e, acc):
            done = [None] * 8
            for m in range(9):
                if m < 8:
                    wait_slab(e, m)
                    t = acc.next("act")
                    wait_emptied(e, t)
                    mm_tile(e, pair(t.s), slabs[:, m], a, KD).then_inc(acc_ready, 1)
                    done[m] = t.out
                if m >= 1:
                    e.eng.wait_ge(*done[m - 1])
                    t = acc.next("dve")
                    wait_emptied(e, t)
                    for half in range(2):
                        last = e.eng.matmul(pair(t.s)[:, half, :], rot, zqk[:, m - 1, half * HALF:(half + 1) * HALF],
                                            start=True, stop=True)
                    last.then_inc(acc_ready, 1)

        def pe_value_rows(e, acc, slot, x):
            for i in range(4):
                wait_slab(e, slot + i)
            for i in range(5):
                n = P if i < 4 else NS
                t = acc.next("act")
                wait_emptied(e, t)
                for k in range(KD):
                    last = e.eng.matmul(psum[0:n, 2 * t.s, :], x[:, k, i * P:i * P + n], slabs[:, slot:slot + 4, k, :],
                                        start=(k == 0), stop=(k == KD - 1))
                last.then_inc(acc_ready, 1)

        def act_value_rows(e, acc, dst, dst_s):
            for i in range(5):
                t = acc.next("act")
                wait_filled(e, t)
                n = P if i < 4 else NS
                e.eng.activation(dst[:, i, :] if i < 4 else dst_s[0:NS, :], psum[0:n, 2 * t.s, :], ACT.Copy)\
                    .then_inc(copied["act"], 1)

        def act_proj_a(e, acc):
            for j in range(5):
                if j < 4:
                    t = acc.next("act")
                    wait_filled(e, t)
                    e.eng.activation(upiece[j % 2][0:NCH].rearrange("p g (s c) -> p s g c", s=CH),
                                     psum[0:NCH, 2 * t.s:2 * t.s + 2, :].rearrange("p b n -> p (b n)")
                                     .rearrange("p (s g c) -> p s g c", s=CH, g=8), ACT.Copy)\
                        .then_inc(copied["act"], 1)
                if j >= 1:
                    t = acc.next("act")
                    wait_filled(e, t)
                    e.eng.activation(halves(uT[:, 8 * (j - 1):8 * j, :].rearrange("p g c -> p (g c)")), pair(t.s),
                                     ACT.Copy).then_inc(copied["act"], 1)
            act_value_rows(e, acc, vt, vs)
            for m in range(9):
                if m < 8:
                    t = acc.next("act")
                    wait_filled(e, t)
                    e.eng.activation(halves(zqk[:, m, :]), pair(t.s), ACT.Copy).then_inc(copied["act"], 1)
                if m >= 1:
                    acc.next("dve")

        def dve_proj_a(e, acc):
            v = e.eng
            acc.skip(13)
            tm = hin_flat[:, 0:T]
            done = [None] * 8
            cos, sin = lcon[:, 0:T], lcon[:, T:2 * T]
            for m in range(9):
                if m < 8:
                    acc.next("act")
                if m >= 1:
                    t = acc.next("dve")
                    wait_filled(e, t)
                    z = zqk[:, m - 1, :]
                    v.tensor_tensor(halves(tm), pair(t.s), halves(sin), ALU.mult).then_inc(copied["dve"], 1)
                    e.st.do(v.tensor_tensor(z, z, cos, ALU.mult))
                    e.st.do(v.tensor_tensor(z, z, tm, ALU.add))

        def sp_proj_a(ld, n):
            for j, at in enumerate((1, 2, 4, 6)):
                ld.load(j, n + at)
            for j in range(4):
                ld.load(4 + j, n + 13)
            for m in range(8):
                ld.load(m, n + 14 + max(0, 2 * m - 1))

        kp_full, mt_zero = sem("kp_full"), sem("mt_zero")
        mt_in = [sem("mt_in0"), sem("mt_in1")]

        def pe_s5_states(e, acc):
            pe = e.eng
            last_copy = None
            for ri in range(2):
                for j in range(2):
                    t = acc.next("act")
                    wait_emptied(e, t)
                    for i in range(8):
                        last = pe.transpose(psum[:, 2 * t.s + i // 4, (i % 4) * P:(i % 4 + 1) * P],
                                            xwt[ri][:, 8 * j + i, :, :], ident)
                    last.then_inc(acc_ready, 1)
                    last_copy = t.out
            pe.wait_ge(*last_copy)
            for ri in range(2):
                for j in range(2):
                    t = acc.next("act")
                    wait_emptied(e, t)
                    for i in range(8):
                        gp = 8 * j + i
                        for g2 in range(2):
                            last = pe.matmul(psum[64 * g2:64 * g2 + 64, 2 * t.s + i // 4, (i % 4) * NCH:(i % 4 + 1) * NCH],
                                             xw[ri][:, gp, 64 * g2:64 * g2 + 64], uT[:, 2 * gp + g2, :],
                                             start=True, stop=True)
                    last.then_inc(acc_ready, 1)
            for j in range(4):
                t = acc.next("act")
                wait_emptied(e, t)
                for g2 in range(2):
                    r0 = 64 * g2
                    for i in range(4):
                        gp = 4 * j + i
                        for ri in range(2):
                            last = pe.matmul(psum[0:SC, 2 * t.s + g2, i * P:(i + 1) * P], bp[ri][r0:r0 + 64, gp, :],
                                             q5[ri][r0:r0 + 64, gp, 0:CH, :], start=(ri == 0), stop=(ri == 1))
                last.then_inc(acc_ready, 1)

        def act_s5_states(e, acc):
            for ri in range(2):
                for j in range(2):
                    t = acc.next("act")
                    wait_filled(e, t)
                    e.eng.activation(xw[ri][:, 8 * j:8 * j + 8, :].rearrange("p (b g) n -> p b (g n)", b=2),
                                     psum[:, 2 * t.s:2 * t.s + 2, :], ACT.Copy).then_inc(copied["act"], 1)
            for ri in range(2):
                for j in range(2):
                    t = acc.next("act")
                    wait_filled(e, t)
                    e.eng.activation(halves(hin[ri][:, 8 * j:8 * j + 8, :].rearrange("p g c -> p (g c)")), pair(t.s),
                                     ACT.Copy).then_inc(copied["act"], 1)
            for j in range(4):
                t = acc.next("act")
                wait_filled(e, t)
                if j >= 2:
                    e.eng.wait_ge(kp_full, j - 1)
                    e.eng.wait_ge(mt_in[j % 2], 16 * CH)
                e.eng.activation(kp[j % 2].rearrange("p (i g) n -> p g i n", g=2),
                                 psum[0:SC, 2 * t.s:2 * t.s + 2, :].rearrange("p g (i n) -> p g i n", i=4),
                                 ACT.Copy).then_inc(copied["act"], 1)

        def dve_s5_states(e, acc):
            v, do = e.eng, e.st.do
            tt = v.tensor_tensor
            xws = [acc.next("act") for _ in range(4)]
            xs = [acc.next("act") for _ in range(4)]
            wait_filled(e, xws[3])
            v.memset(mt_all, 0.0).then_inc(mt_zero, 1)
            cmulp = lambda o, x: cmul(e, o, x, x, [u0, u1])
            cmulp([cs, sn], [cs, sn])
            cmulp([cs, sn], [cs, sn])
            cmulp([cs, sn], [cs, sn])
            do(v.memset(ph[0][:, :, 0:1], 1.0))
            do(v.memset(ph[1][:, :, 0:1], 0.0))
            n = 1
            while n < NC_P:
                step = [x.unsqueeze(2).to_broadcast([P, GP, n]) for x in (cs, sn)]
                temps = [z[:, 0:GP * n].rearrange("p (g c) -> p g c", g=GP) for z in (a_sb[:, 4096:4608], rstd)]
                cmul(e, [z[:, :, n:2 * n] for z in ph], [z[:, :, 0:n] for z in ph], step, temps)
                n *= 2
                if n < NC_P:
                    cmulp([cs, sn], [cs, sn])
            for j in range(4):
                t = acc.next("act")
                v.wait_ge(*t.out)
                if j:
                    v.wait_ge(kp_full, j)
                do(tt(dpass, ident[0:SC, 0:SC].unsqueeze(1).to_broadcast([SC, 8, SC]),
                      d16[:, 8 * j:8 * j + 8].unsqueeze(2).to_broadcast([SC, 8, SC]), ALU.mult))
                tt(kp[j % 2][:, :, 0:SC], kp[j % 2][:, :, 0:SC], dpass, ALU.add).then_inc(kp_full, 1)
            v.wait_ge(kp_full, 4)
            v.wait_ge(*xs[3].out)
            p8 = [z[:, :, CH:CH + 1].to_broadcast([P, GP, NB]) for z in powr]
            so = [z[:, :, 1:9] for z in s5o]
            cmul(e, so, st0, p8, [z[:, :, 0:NB] for z in tmp5])
            for z, x in zip(so, hin):
                do(tt(z, z, x[:, :, NC_P:NCH], ALU.add))
            cmul(e, gst, [x[:, :, 0:NC_P] for x in hin], ph, tmp5, conj=True)
            do(v.tensor_copy(tmp5[0], mag8.unsqueeze(2).to_broadcast([P, GP, NC_P])))
            do(v.memset(tmp5[0][:, :, 0:1], 0.0))
            for z in gst:
                f = z.rearrange("p g c -> p (g c)")
                do(v.tensor_tensor_scan(out=f, data0=tmp5[0].rearrange("p g c -> p (g c)"), data1=f, initial=0.0,
                                        op0=ALU.mult, op1=ALU.add))
            cmul(e, gst, gst, ph, tmp5)
            for z, x, o, s in zip(gst, hin, s5o, st0):
                do(v.tensor_copy(x[:, :, 1:NC_P], z[:, :, 0:NC_P - 1]))
                do(v.memset(x[:, :, 0:1], 0.0))
                do(v.tensor_copy(x[:, :, NC_P:NCH], s))
                do(v.tensor_copy(o[:, :, 0:1], z[:, :, NC_P - 1:NC_P]))

        def sp_s5_states(ld):
            ld.sp.wait_ge(mt_zero, 1)
            for j in range(4):
                ld.sp.wait_ge(kp_full, j + 1)
                for s in range(CH):
                    ld.sp.dma_start(mt[SC * s:SC * s + SC, 8 * j:8 * j + 8, SC * s:P], kp[j % 2][:, :, 0:P - SC * s])\
                        .then_inc(mt_in[j % 2], 16)

        def pe_s5_out(e, acc):
            pe = e.eng
            for s in mt_in:
                pe.wait_ge(s, 16 * 2 * CH)
            piece_copied = [None] * 4
            for j in range(5):
                if j < 4:
                    t = acc.next("act")
                    wait_emptied(e, t)
                    for g2 in range(2):
                        r0 = 64 * g2
                        for i in range(4):
                            gp = 4 * j + i
                            o = psum[0:NCH, 2 * t.s + g2, i * P:(i + 1) * P]
                            pe.matmul(o, uT[:, 2 * gp + g2, :], mt[:, 2 * gp + g2, :], start=True, stop=False)
                            for ri in range(2):
                                last = pe.matmul(o, hin[ri][r0:r0 + 64, gp, :], q5[ri][r0:r0 + 64, gp, 1:CH + 1, :],
                                                 start=False, stop=(ri == 1))
                    last.then_inc(acc_ready, 1)
                    piece_copied[j] = (copied["act"], t.out[1] + 1)
                    acc.count["act"] += 1
                    acc.last[t.s] = piece_copied[j]
                if j >= 1:
                    pe.wait_ge(*piece_copied[j - 1])
                    t = acc.next("act")
                    wait_emptied(e, t)
                    for st in range(CH):
                        last = pe.transpose(psum[:, 2 * t.s + st // 4, (st % 4) * NCH:(st % 4 + 1) * NCH],
                                            piece[(j - 1) % 2][0:NCH, st, :], ident[0:NCH, 0:NCH])
                    last.then_inc(acc_ready, 1)

        def s5_out_tiles(acc):
            for j in range(5):
                if j < 4:
                    t = acc.next("act")
                    acc.count["act"] += 1
                    acc.last[t.s] = (copied["act"], acc.count["act"])
                    yield "piece", j, t
                if j >= 1:
                    yield "turned", j - 1, acc.next("act")

        def act_s5_out(e, acc):
            for what, j, t in s5_out_tiles(acc):
                wait_filled(e, t)
                if what == "piece":
                    for g2 in range(2):
                        dst = piece[j % 2][0:NCH].rearrange("p s (i g c) -> p g i s c", g=2, c=SC)[:, g2]
                        e.eng.activation(dst, psum[0:NCH, 2 * t.s + g2, :].rearrange("p (i s c) -> p i s c", i=4, s=CH),
                                         ACT.Gelu_apprx_tanh).then_inc(copied["act"], 1)
                else:
                    e.eng.activation(y[:, j, :].rearrange("p (c b s) -> p b s c", b=2, s=4),
                                     pair(t.s).rearrange("p b (s c) -> p b s c", s=4),
                                     ACT.Copy).then_inc(copied["act"], 1)

        def pe_glu(e, acc):
            for m in range(4):
                if m % 2 == 0:
                    wait_slab(e, m // 2)
                t = acc.next("act")
                wait_emptied(e, t)
                mm_tile(e, pair(t.s), slabs[:, m // 2, 4 * (m % 2):4 * (m % 2) + 4], y, 4).then_inc(acc_ready, 1)

        def act_glu(e, acc):
            for m in range(4):
                t = acc.next("act")
                wait_filled(e, t)
                e.eng.activation(halves(sgate[:, m, :]), pair(t.s), ACT.Sigmoid, bias=vcol(0, "b_glu", m))\
                    .then_inc(copied["act"], 1)

        def dve_glu(e, acc):
            for m in range(4):
                t = acc.next("act")
            wait_filled(e, t)
            e.eng.wait_ge(*t.out)
            for m in range(4):
                e.eng.tensor_tensor(y[:, m, :], y[:, m, :], sgate[:, m, :], ALU.mult)

        mt_all = cut(mt_at, GRP * P)
        dpass = arena[0:SC, tiny_at + 17 * GP:tiny_at + 17 * GP + 8 * SC].rearrange("p (g c) -> p g c", g=8)
        sgate = uT_flat.rearrange("p (m t) -> p m t", m=4)

        S5_LOADS = [(ar, "s5_ar"), (ai, "s5_ai"), (ldt, "s5_ldt"), (cut(bc_at, 1024), "s5_bc"), (d16, "s5_d"),
                    (cut(st_at, 256), "s5_st")]
        _c[0] = mixer_free
        kv_at = take(2 * NPG * 512)
        tmp_at = kv_at + 2 * NPG * 512
        kv = [z.rearrange("p (g n) -> p g n", g=NPG) for z in (
            cut(kv_at, NPG * 512), cut(kv_at + NPG * 512, NPG * 512),
            ring[:, RAW * SLAB:RING * SLAB], a_sb[:, 0:NPG * 512])]

        NPAIR = NB // 2
        KEYS = PAST + NS
        _c[0] = tmp_at
        qz_at = take(4 * NPAIR * 2 * 32)
        qz_flat = cut(qz_at, 4 * NPAIR * 2 * 32)
        qz = qz_flat.rearrange("p (c i s x) -> p c i s x", c=4, i=NPAIR, s=2)
        wz = cut(take(KEYS), KEYS)
        we = cut(take(KEYS), KEYS)
        wt = cut(take(9 * P), 9 * P).rearrange("p (g n) -> p g n", g=9)
        osb = cut(take(2 * P), 2 * P)
        sst = cut(take(40), 40)
        unit_at = _c[0]
        s_new, s_newt, s_out = psum[:, 7, 0:NS], psum[0:NS, 7, NS:NS + P], psum[:, 7, NS + P:NS + 3 * P]

        def between(pieces, u, last, due):
            apart, units = due
            for x in range(u, 8 * NPAIR + 16) if u == last else [u]:
                for i, p in enumerate(pieces):
                    for d in units:
                        if apart * i + d == x:
                            next(p, None)

        kv_in = [sem(f"kv_in{i}") for i in range(4)]
        queries, k_used, v_used, z_copied, bias_ready, sw_ready, wt_full, wt_ready, o_scaled, ot_full, y_copied = (
            sem(x) for x in ("queries", "k_used", "v_used", "z_copied", "bias_ready", "sw_ready", "wt_full", "wt_ready",
                             "o_scaled", "ot_full", "y_copied"))
        neg_ready, soft_ready, sub_ready = sem("neg_ready"), sem("soft_ready"), sem("sub_ready")

        def sp_stream(eng, keys, values, layer):
            def pair_of(i, n):
                ids = [[eng.value_load(pages[0:1, bass.ds((2 * i + s) * NPG + g, 1)], min_val=0,
                                       max_val=keys.shape[0] - 1) for g in range(NPG)] for s in range(2)]
                for cache, at, used in ((keys, 0, k_used), (values, 2, v_used)):
                    for s in range(2):
                        if n is not None:
                            eng.wait_ge(used, n + s)
                        for g in range(NPG):
                            src = cache[bass.ds(ids[s][g], 1)]
                            src = src.rearrange("a p n -> p (a n)") if len(cache.shape) == 3 else \
                                src.rearrange("a p c n -> p (a c n)")
                            eng.dma_start(kv[at + s][:, g, :], src).then_inc(kv_in[at + s], 16)

            pair_of(0, NB * layer - 1 if layer else None)
            with eng.Fori(1, NPAIR) as i:
                pair_of(i, NB * layer - 1 + 2 * i)

        def pe_sample_pair(e, layer, i):
            pe = e.eng
            n = NPAIR * layer + i
            if i == 0:
                pe.wait_ge(queries, layer + 1)
            for s in range(2):
                pe.wait_ge(kv_in[s], 16 * NPG * (n + 1))
                keys = kv[s].rearrange("p g (c n) -> p g c n", c=4)
                for half in range(2):
                    for c in range(4):
                        last = pe.matmul(psum[32 * c:32 * c + 32, 5 + half, :], qz[:, c, i, s, :],
                                         keys[:, 4 * half:4 * half + 4, c, :], start=(s == 0), stop=(s == 1))
                if s == 1:
                    if n >= 1:
                        pe.wait_ge(y_copied, n)
                    for z in range(2):
                        for c in range(4):
                            last = pe.matmul(s_new[32 * c:32 * c + 32], qz[:, c, i, z, :], zqk[:, 4 + c, TP:T],
                                             start=(z == 0), stop=(z == 1))
                last.then_inc(k_used, 1)
                yield
            pe.wait_ge(sw_ready, n + 1)
            for g in range(NPG):
                pe.transpose(psum[:, 5 + g // 4, (g % 4) * P:(g % 4 + 1) * P], wz[:, g * P:(g + 1) * P], ident)
            pe.transpose(s_newt, wz[:, PAST:KEYS], ident).then_inc(wt_full, 1)
            yield
            pe.wait_ge(wt_ready, n + 1)
            for s in range(2):
                pe.wait_ge(kv_in[2 + s], 16 * NPG * (n + 1))
                for g in range(NPG + 1):
                    rows = P if g < NPG else NS
                    v = kv[2 + s][:, g, :] if g < NPG else vs
                    for c in range(4):
                        last = pe.matmul(s_out[32 * c:32 * c + 32, s * P:(s + 1) * P],
                                         wt[0:rows, g, 32 * c:32 * c + 32], v[0:rows, c * P:(c + 1) * P],
                                         start=(g == 0), stop=(g == NPG))
                last.then_inc(v_used, 1)
                yield
            pe.wait_ge(o_scaled, n + 1)
            for s in range(2):
                last = pe.transpose(s_out[:, s * P:(s + 1) * P], osb[:, s * P:(s + 1) * P], ident)
            last.then_inc(ot_full, 1)
            yield

        def act_turned(e, n):
            act = e.eng
            act.wait_ge(wt_full, n + 1)
            if n >= 1:
                act.wait_ge(v_used, 2 * n)
            act.activation(wt[:, 0:NPG, :].rearrange("p (a g) n -> p a (g n)", a=2), psum[:, 5:7, :], ACT.Copy)
            act.activation(wt[0:NS, NPG, :], s_newt, ACT.Copy).then_inc(wt_ready, 1)

        def dve_queries(e):
            v = e.eng
            e.st.do(v.memset(qz_flat, 0.0))
            q = zqk[:, 0:4, TP:T].rearrange("p c (i s t) -> p c i s t", s=2, t=TS)
            for s in range(2):
                for g in range(2):
                    at = 16 * s + 8 * g
                    e.st.do(v.tensor_copy(qz[64 * g:64 * g + 64, :, :, s, at:at + TS], q[64 * g:64 * g + 64, :, :, s, :]))
            v.drain().then_inc(queries, 1)

        def dve_outputs(e, i, n, rden):
            v = e.eng
            v.wait_ge(v_used, 2 * n + 2)
            if n >= 1:
                v.wait_ge(ot_full, n)
            if rden is None:
                v.tensor_copy(osb, s_out).then_inc(o_scaled, 1)
            else:
                v.tensor_scalar(osb, s_out, rden, None, ALU.mult).then_inc(o_scaled, 1)
            yield
            v.wait_ge(ot_full, n + 1)
            for s in range(2):
                for g in range(2):
                    at = TP + (2 * i + s) * TS
                    o = s_out[64 * g:64 * g + 64, s * P:(s + 1) * P].rearrange("p (c x) -> p c x", c=4)
                    last = v.tensor_copy(y[64 * g:64 * g + 64, 4:8, at:at + TS], o[:, :, 16 * s + 8 * g:16 * s + 8 * g + TS])
            last.then_inc(y_copied, 1)
            yield

        pb = [cut(unit_at + i * 512, 512) for i in range(2)]
        ptb = [cut(unit_at + (2 + i) * 512, 512).rearrange("p (j n) -> p j n", j=4) for i in range(2)]
        stat = small[:, 8:64]

        sco_ready, nmx_ready, prob_ready, pn_ready, ptr_ready, pt_ready, o_unit, o_copied = (
            sem(x) for x in ("sco_ready", "nmx_ready", "prob_ready", "pn_ready", "ptr_ready", "pt_ready", "o_unit", "o_copied"))
        UNITS = [(hh, i) for hh in range(NH) for i in range(4)]
        DUE_A = {"pe": (6, (4, 7, 9, 10, 11, 12)), "act": (6, (8, 9)), "dve": (6, (8, 11, 12))}

        def pe_moba_prompt(e):
            pe = e.eng
            samples = [pe_sample_pair(e, 0, i) for i in range(NPAIR)]
            for u in range(len(UNITS) + 2):
                if u < len(UNITS):
                    hh, i = UNITS[u]
                    r0, c, n = 64 * (hh % 2), hh // 2, P * (i + 1)
                    if u >= 2:
                        pe.wait_ge(prob_ready, u - 1)
                    pe.matmul(psum[:, u % 2, 0:n], zqk[r0:r0 + 64, c, i * P:(i + 1) * P], zqk[r0:r0 + 64, 4 + c, 0:n],
                              start=True, stop=True).then_inc(sco_ready, 1)
                if 1 <= u <= len(UNITS):
                    hh, i = UNITS[u - 1]
                    pe.wait_ge(pn_ready, u)
                    if u >= 3:
                        pe.wait_ge(pt_ready, u - 2)
                    for j in range(i + 1):
                        last = pe.transpose(psum[:, 2 + (u - 1) % 2, j * P:(j + 1) * P],
                                            pb[(u - 1) % 2][:, j * P:(j + 1) * P], ident)
                    last.then_inc(ptr_ready, 1)
                if u >= 2:
                    hh, i = UNITS[u - 2]
                    r0, c = 64 * (hh % 2), hh // 2
                    pe.wait_ge(pt_ready, u - 1)
                    if hh % 2 == 0 and i == 0 and c >= 1:
                        pe.wait_ge(o_copied, c)
                    for j in range(i + 1):
                        last = pe.matmul(psum[r0:r0 + 64, 4, i * P:(i + 1) * P],
                                         vt[:, j, hh * HD:(hh + 1) * HD], ptb[u % 2][:, j, :],
                                         start=(j == 0), stop=(j == i))
                    last.then_inc(o_unit, 1)
                between(samples, u, len(UNITS) + 1, DUE_A["pe"])

        def act_moba_prompt(e):
            act = e.eng

            def copy_out(c):
                act.wait_ge(o_unit, 8 * (c + 1))
                act.activation(y[:, 4 + c, 0:TP], psum[:, 4, :], ACT.Copy).then_inc(o_copied, 1)

            act.wait_ge(stored, 16 * 5)
            act.preload_act_table_set("natural_log_exp_and_others")
            samples = [act_moba_sample(e, i) for i in range(NPAIR)]
            for u in range(len(UNITS) + 1):
                if u < len(UNITS):
                    hh, i = UNITS[u]
                    n = P * (i + 1)
                    act.wait_ge(nmx_ready, u + 1)
                    if u >= 2:
                        act.wait_ge(ptr_ready, u - 1)
                    act.activation(pb[u % 2][:, 0:n], psum[:, u % 2, 0:n], ACT.Exp, scale=ATT_SCALE,
                                   bias=stat[:, 2 + u % 2:3 + u % 2], accum_out=stat[:, 4 + u % 2:5 + u % 2])\
                       .then_inc(prob_ready, 1)
                if u >= 1:
                    hh, i = UNITS[u - 1]
                    act.wait_ge(ptr_ready, u)
                    if u >= 3:
                        act.wait_ge(o_unit, u - 2)
                    act.activation(ptb[(u - 1) % 2][:, 0:i + 1, :], psum[:, 2 + (u - 1) % 2, 0:P * (i + 1)]
                                   .rearrange("p (j n) -> p j n", j=i + 1), ACT.Copy).then_inc(pt_ready, 1)
                if u >= 9 and (u - 9) % 8 == 0:
                    copy_out((u - 9) // 8)
                if u == len(UNITS):
                    copy_out(3)
                between(samples, u, len(UNITS), DUE_A["act"])

        def dve_moba_prompt(e):
            v, do = e.eng, e.st.do
            v.wait_ge(stored, 16 * 5)
            dve_queries(e)
            samples = [dve_moba_sample(e, i) for i in range(NPAIR)]
            causal = lcon[:, LCON[0]["causal"]:LCON[0]["causal"] + P]
            for u in range(len(UNITS) + 1):
                if u >= 1:
                    w = u - 1
                    n = P * (UNITS[w][1] + 1)
                    v.wait_ge(prob_ready, w + 1)
                    do(v.reciprocal(stat[:, 6 + w % 2:7 + w % 2], stat[:, 4 + w % 2:5 + w % 2]))
                    v.tensor_scalar(pb[w % 2][:, 0:n], pb[w % 2][:, 0:n], stat[:, 6 + w % 2:7 + w % 2], None, ALU.mult)\
                     .then_inc(pn_ready, 1)
                if u < len(UNITS):
                    hh, i = UNITS[u]
                    n = P * (i + 1)
                    v.wait_ge(sco_ready, u + 1)
                    own = psum[:, u % 2, i * P:n]
                    do(v.tensor_tensor(own, own, causal, ALU.add))
                    do(v.tensor_reduce(stat[:, u % 2:u % 2 + 1], psum[:, u % 2, 0:n], AXX, ALU.max))
                    if u >= 2:
                        v.wait_ge(prob_ready, u - 1)
                    v.tensor_scalar(stat[:, 2 + u % 2:3 + u % 2], stat[:, u % 2:u % 2 + 1], -ATT_SCALE, None, ALU.mult)\
                     .then_inc(nmx_ready, 1)
                between(samples, u, len(UNITS), DUE_A["dve"])

        def act_moba_sample(e, i):
            act, w, m = e.eng, wz, sst
            act.wait_ge(bias_ready, i + 1)
            for j in range(4):
                act.activation(w[:, 256 * j:256 * j + 256], psum[:, 5 + j // 2, 256 * (j % 2):256 * (j % 2) + 256],
                               ACT.Exp, scale=ATT_SCALE, bias=m[:, 20 + j:21 + j], accum_out=m[:, 24 + j:25 + j])
            act.activation(w[:, PAST:KEYS], w[:, PAST:KEYS], ACT.Exp, bias=m[:, 19:20], accum_out=m[:, 28:29])\
               .then_inc(sw_ready, 1)
            yield
            act_turned(e, i)
            yield

        def dve_moba_sample(e, i):
            v, do, w, m = e.eng, e.st.do, wz, sst
            tt = v.tensor_tensor
            sums, eq, late, pen, mx, nmx, bias, den = (m[:, 0:4], m[:, 4:8], m[:, 8:12], m[:, 12:16], m[:, 30:36],
                                                       m[:, 19:20], m[:, 20:24], m[:, 24:29])
            v.wait_ge(k_used, 2 * i + 2)
            if i >= 1:
                v.wait_ge(wt_full, i)
            new = lcon[:, LCON[0]["new"] + NS * i:LCON[0]["new"] + NS * (i + 1)]
            do(v.scalar_tensor_tensor(w[:, PAST:KEYS], s_new, ATT_SCALE, new, ALU.mult, ALU.add))
            blocks = psum[:, 5:7, :].rearrange("p b n -> p (b n)").rearrange("p (j x) -> p j x", j=4)
            do(v.tensor_reduce(sums, blocks, AXX, ALU.add))
            do(v.tensor_reduce(mx[:, 0:4], blocks, AXX, ALU.max))
            do(v.tensor_reduce(mx[:, 4:5], w[:, PAST:KEYS], AXX, ALU.max))
            do(v.tensor_reduce(m[:, 16:17], sums, AXX, ALU.min))
            do(v.tensor_scalar(eq, sums, m[:, 16:17], None, ALU.is_le))
            do(v.memset(late[:, 3:4], 0.0))
            for j in (2, 1, 0):
                do(tt(late[:, j:j + 1], late[:, j + 1:j + 2], eq[:, j + 1:j + 2], ALU.max))
            do(tt(eq, eq, late, ALU.is_gt))
            do(v.tensor_scalar(pen, eq, NEG, None, ALU.mult))
            do(v.scalar_tensor_tensor(mx[:, 0:4], mx[:, 0:4], ATT_SCALE, pen, ALU.mult, ALU.add))
            do(v.tensor_reduce(m[:, 17:18], mx[:, 0:5], AXX, ALU.max))
            do(v.tensor_scalar(nmx, m[:, 17:18], -1.0, None, ALU.mult))
            v.tensor_scalar(bias, pen, nmx, None, ALU.add).then_inc(bias_ready, 1)
            yield
            v.wait_ge(sw_ready, i + 1)
            do(v.tensor_reduce(m[:, 18:19], den, AXX, ALU.add))
            do(v.reciprocal(m[:, 29:30], m[:, 18:19]))
            yield from dve_outputs(e, i, i, m[:, 29:30])

        ff = cut(0, FT * T).rearrange("p (m t) -> p m t", m=FT)
        _c[0] = FT * T
        TU = 2 + TP + NB * (2 + TS)
        ub = [cut(take(TU), TU) for _ in range(4)]
        cb = [cut(take(T), T) for _ in range(4)]
        fst = cut(take(2 * FT * NB * 2), 2 * FT * NB * 2).rearrange("p (m b j) -> p m b j", m=2 * FT, b=NB)
        fo_at = take(2 * FT * 18)
        fo = cut(fo_at, 2 * FT * 18).rearrange("p (m x) -> p m x", m=2 * FT)
        assert _c[0] <= ARENA, _c[0]
        ptile = cut(0, 2 * T).rearrange("p (k t) -> p k t", k=2)

        fst_in, pt_in, pw_in = sem("fst_in"), sem("pt_in"), sem("pw_in")
        conv_a, conv_d, geg_ready, x_new = sem("conv_a"), sem("conv_d"), sem("geg_ready"), sem("x_new")

        def pe_dense_split(e, acc, tiles, x, off=0):
            for m in range(tiles):
                e.splits += 1
                e.eng.wait_ge(wl_ready, e.splits)
                t = acc.next("act")
                wait_emptied(e, t)
                mm_split(e, pair(t.s), split[(m + off) % 4], x, KD, x_parts=e.parts if m == 0 else None)\
                    .then_inc(acc_ready, 1)
            e.parts += KD

        def act_split_first(e):
            for n in range(AHEAD):
                act_split_slab(e, n, None)

        def dve_split_first(e):
            for n in range(AHEAD):
                dve_split_slab(e, n)

        def act_dense_split(e, acc, tiles, dst, func=lambda m: ACT.Copy, off=0):
            n0 = acc.n
            for m in range(tiles):
                if m + AHEAD < tiles:
                    act_split_slab(e, m + AHEAD, n0 + m + AHEAD - 3 if m + AHEAD >= 4 else None, off)
                t = acc.next("act")
                wait_filled(e, t)
                e.eng.activation(halves(dst(m)), pair(t.s), func(m)).then_inc(copied["act"], 1)

        def dve_dense_split(e, tiles):
            for m in range(AHEAD, tiles):
                dve_split_slab(e, m)

        def sp_split_first(ld):
            ld.begin_split()
            for _ in range(RAW):
                ld.load_raw()

        def sp_dense_split(ld, tiles, last):
            for _ in range(tiles - RAW):
                ld.load_raw()
            ld.end_split(last)

        ROUNDS = 2 * FT // RING
        REST = (2 * FT % RING) // 2

        def pe_up(e, acc):
            pe = e.eng
            n0, c0, w0 = acc.n, acc.count["act"], e.splits

            def tiles(i, count):
                for j in range(count):
                    pe.wait_ge(wl_ready, w0 + j + 1 + i * RING)
                    pe.wait_ge(copied["act"], c0 + j - 3 + i * RING)
                    first = isinstance(i, int) and i == 0 and j == 0
                    mm_split(e, pair((n0 + j) % 4), split[j % 4], (a, y), KD, x_parts=e.parts if first else None)\
                        .then_inc(acc_ready, 1)

            tiles(0, RING)
            with pe.Fori(1, ROUNDS) as i:
                tiles(i, RING)
            tiles(ROUNDS, 2 * REST)
            e.splits += 2 * FT
            e.parts += KD
            acc.skip(2 * FT)

        def act_up(e, acc):
            act = e.eng
            n0 = acc.n
            g0 = e.ups * FT
            raws = list(e.raws)
            for n in range(AHEAD):
                raws[n % RAW] -= 1

            def split_slab(i, n):
                act.wait_ge(raw_in[n % RAW], 16 * (raws[n % RAW] + 1 + n // RAW) + i * (16 * RING // RAW))
                act.wait_ge(acc_ready, n0 + n - 3 + i * RING)
                act_high(e, slabs[:, n % RAW], split[n % 4][0], wh_ready)

            def pairs_of(i, count):
                for j in range(count):
                    pr = 4 * i + j
                    for v in range(2):
                        if not isinstance(i, int) or 8 * i + 2 * j + v + AHEAD < 2 * FT:
                            split_slab(i, 2 * j + v + AHEAD)
                        s = (n0 + 2 * j + v) % 4
                        u = ub[2 * (j % 2) + v]
                        act.wait_ge(acc_ready, n0 + 2 * j + v + 1 + i * RING)
                        if v == 0 and not (isinstance(i, int) and i == 0 and j < 2 and e.ups == 0):
                            act.wait_ge(geg_ready, g0 + j - 1 + i * 4)
                        act.activation(u[:, 2:2 + HALF], psum[:, 2 * s, 0:HALF], ACT.Copy)
                        act.activation(u[:, 2 + HALF:2 + TP], psum[:, 2 * s + 1, 0:TP - HALF], ACT.Copy)
                        act.activation(u[:, 2 + TP:TU].rearrange("p (b t) -> p b t", b=NB)[:, :, 2:],
                                       psum[:, 2 * s + 1, TP - HALF:HALF].rearrange("p (b t) -> p b t", b=NB), ACT.Copy)\
                           .then_inc(copied["act"], 1)
                    act.wait_ge(conv_d, g0 + j + 1 + i * 4)
                    act.activation(cb[2 * (j % 2)], cb[2 * (j % 2)], ACT.Gelu_apprx_tanh).then_inc(conv_a, 1)

            pairs_of(0, 4)
            with act.Fori(1, ROUNDS) as i:
                pairs_of(i, 4)
            pairs_of(ROUNDS, REST)
            e.raws = [x + 2 * FT // RAW for x in raws]
            acc.skip(2 * FT)
            e.ups += 1

        def dve_up(e, acc, layer):
            v = e.eng
            c0 = acc.count["act"]
            g0 = e.ups * FT
            base = layer * NVEC
            w0 = e.splits - AHEAD
            v.wait_ge(fst_in, 16 * (layer + 1))

            def pairs_of(i, count):
                for j in range(count):
                    for w in range(2):
                        n = 2 * j + w + AHEAD
                        if not isinstance(i, int) or 8 * i + n < 2 * FT:
                            v.wait_ge(wh_ready, w0 + n + 1 + i * RING)
                            dve_low(e, slabs[:, n % RAW], split[n % 4][0], split[n % 4][1], wl_ready)
                        u, cv = ub[2 * (j % 2) + w], cb[2 * (j % 2) + w]
                        m = 4 * i + j + FT * w
                        us = u[:, 2 + TP:TU].rearrange("p (b t) -> p b t", b=NB)
                        e.st.do(v.tensor_copy(us[:, :, 0:2], fst[:, bass.ds(m, 1), :, :].rearrange("p m b j -> p (m b) j")))
                        v.wait_ge(copied["act"], c0 + 2 * j + w + 1 + i * RING)
                        tap = [vec[:, bass.ds(base + VEC[x] + m, 1)] for x in ("conv0", "conv1", "conv2", "conv_b")]
                        cs_ = cv[:, TP:T].rearrange("p (b t) -> p b t", b=NB)
                        v.tensor_scalar(cv[:, 0:TP], u[:, 0:TP], tap[0], tap[3], ALU.mult, ALU.add)
                        e.st.do(v.tensor_scalar(cs_, us[:, :, 0:TS], tap[0], tap[3], ALU.mult, ALU.add))
                        v.scalar_tensor_tensor(cv[:, 0:TP], u[:, 1:1 + TP], tap[1], cv[:, 0:TP], ALU.mult, ALU.add)
                        e.st.do(v.scalar_tensor_tensor(cs_, us[:, :, 1:1 + TS], tap[1], cs_, ALU.mult, ALU.add))
                        v.scalar_tensor_tensor(cv[:, 0:TP], u[:, 2:2 + TP], tap[2], cv[:, 0:TP], ALU.mult, ALU.add)
                        last = v.scalar_tensor_tensor(cs_, us[:, :, 2:2 + TS], tap[2], cs_, ALU.mult, ALU.add)
                        if w == 0:
                            last.then_inc(conv_d, 1)
                        else:
                            e.st.do(last)
                        o = fo[:, bass.ds(m, 1), :].rearrange("p m x -> p (m x)")
                        v.tensor_copy(o[:, 0:2], u[:, TP:2 + TP])
                        e.st.do(v.tensor_copy(o[:, 2:18].rearrange("p (b j) -> p b j", j=2), us[:, :, TS:TS + 2]))
                    v.wait_ge(conv_a, g0 + j + 1 + i * 4)
                    v.tensor_tensor(ff[:, bass.ds(4 * i + j, 1), :].rearrange("p m t -> p (m t)"), cb[2 * (j % 2)],
                                    cb[2 * (j % 2) + 1], ALU.mult).then_inc(geg_ready, 1)

            for u in ub:
                e.st.do(v.memset(u[:, 0:2], 0.0))
            with v.Fori(0, ROUNDS) as i:
                e.st.enter(i, 4 * 2 * 5 - 4)
                pairs_of(i, 4)
                e.st.leave(ROUNDS)
            pairs_of(ROUNDS, REST)
            e.splits = w0 + 2 * FT
            acc.skip(2 * FT)
            e.ups += 1

        def sp_up(ld, n0):
            sp = ld.sp
            ld.begin_split()
            for j in range(RING):
                ld.load_raw()
            row, w0 = ld.row - RING, ld.splits - RING
            with sp.Fori(1, ROUNDS) as i:
                for j in range(RING):
                    sp.wait_ge(wl_ready, w0 + j + 1 - RAW + i * RING)
                    sp.dma_start(slabs[:, j % RAW], A["w8"][bass.ds(row + j + i * RING, 1)]
                                 .rearrange("a p (k n) -> p (a k) n", k=KD)).then_inc(raw_in[j % RAW], 16)
            ld.row += RING * (ROUNDS - 1)
            ld.splits += RING * (ROUNDS - 1)
            for slot in range(RAW):
                ld.until[slot * KD:(slot + 1) * KD] = [(wl_ready, ld.splits - RAW + slot + 1)] * KD
            for j in range(2 * REST):
                ld.load_raw()
            ld.end_split(n0 + 2 * FT)

        ffh = cut(FT * T, FT * T).rearrange("p (m t) -> p m t", m=FT)

        def pe_down(e, acc):
            for m in range(KD):
                t = acc.next("act")
                wait_emptied(e, t)
                for part in range(2):
                    e.splits += 1
                    e.eng.wait_ge(wl_ready, e.splits)
                    x = [z[:, 11 * part:11 * part + 11, :] for z in (ffh, ff)]
                    last = mm_split(e, pair(t.s), dsplit[part], x, 11, first=(part == 0), last=(part == 1),
                                    x_parts=e.parts + 11 * part if m == 0 else None)
                    last.then_inc(part_done if part == 0 else acc_ready, 1)
            e.parts += FT

        def act_split_down(e, n, used=None):
            slot = n % DRING
            e.eng.wait_ge(draw_in[slot], 16 * (e.downs * ((2 * KD + DRING - 1 - slot) // DRING) + n // DRING + 1))
            if used is not None:
                e.eng.wait_ge(*used)
            act_high(e, dslabs[:, slot], dsplit[n % 2][0], wh_ready)

        def act_down(e, acc):
            for n in range(2):
                act_split_down(e, n)
            k0 = (fo_at - FT * T) // T
            act_split_rhs(e, tiles_of(ff, k0), tiles_of(ffh, k0))
            e.eng.wait_ge(stored, 16 * (6 if e.downs == 0 else 12))
            act_split_rhs(e, tiles_of(ff, FT)[k0:], tiles_of(ffh, FT)[k0:])
            for m in range(KD):
                t = acc.next("act")
                if m < KD - 1:
                    act_split_down(e, 2 * m + 2, (part_done, KD * e.downs + m + 1))
                    act_split_down(e, 2 * m + 3, (acc_ready, t.n))
                wait_filled(e, t)
                e.eng.activation(halves(a[:, m, :]), pair(t.s), ACT.Copy).then_inc(copied["act"], 1)
            e.downs += 1

        def dve_down(e, acc):
            def low(n):
                e.splits += 1
                e.eng.wait_ge(wh_ready, e.splits)
                dve_low(e, dslabs[:, n % DRING], *dsplit[n % 2], wl_ready)

            for n in range(2):
                low(n)
            dve_split_rhs(e, tiles_of(ff, FT), tiles_of(ffh, FT), tiles_of(ff, FT))
            for n in range(2, 2 * KD):
                low(n)
            acc.skip(KD)

        def sp_down(ld, last):
            for n in range(2 * KD):
                ld.load_down(n)
            ld.until[DRING * 11:] = [(acc_ready, last)] * (RING * KD - DRING * 11)

        yh = cut(0, KD * T).rearrange("p (k t) -> p k t", k=KD)
        plew = cut(4096, 2 * SLAB).rearrange("p (s k n) -> p s k n", s=2, k=KD)
        pproj = cut(8192 + 2 * KD * T, KD * T).rearrange("p (k t) -> p k t", k=KD)
        assert 8192 + 3 * KD * T <= ARENA - 4 * SLAB
        hh_, hl_ = (cut(8192 + i * KD * T, KD * T).rearrange("p (k t) -> p k t", k=KD) for i in range(2))

        def pe_layer_end(e, acc):
            pe_dense_split(e, acc, KD, (yh, y))
            e.fence()
            pe_norm(e, acc, y)
            pe_norm(e, acc, a)
            e.pre += 1
            pe_up(e, acc)
            e.fence()
            pe_down(e, acc)
            e.fence()
            pe_norm(e, acc, y)
            e.eng.wait_ge(pt_in, 16 * e.layer)
            e.eng.wait_ge(pw_in, 32 * e.layer)
            for m in range(KD):
                t = acc.next("act")
                wait_emptied(e, t)
                mm_tile(e, pair(t.s), plew[:, m // 4, 2 * (m % 4):2 * (m % 4) + 2], ptile, 2).then_inc(acc_ready, 1)
            pe_dense_split(e, acc, KD, (hh_, hl_))
            e.fence()
            pe_norm(e, acc, y)
            e.layer += 1

        def act_pre_norm(e, acc):
            act_norm(e, acc, h, a, fresh=True)
            act_split_rhs(e, tiles_of(y), tiles_of(a), after=(x_new, KD * e.pre))
            e.pre += 1

        def dve_pre_norm(e, acc, layer, gain):
            dve_norm(e, acc, h, y, layer, gain, ready=x_new)
            dve_split_rhs(e, tiles_of(y), tiles_of(a), tiles_of(y))

        def act_layer_end(e, acc, layer):
            act_split_first(e)
            act_split_rhs(e, tiles_of(y), tiles_of(yh))
            act_dense_split(e, acc, KD, lambda m: a[:, m, :])
            e.fence()
            act_norm(e, acc, a, y)
            act_split_first(e)
            act_pre_norm(e, acc)
            act_up(e, acc)
            e.fence()
            act_down(e, acc)
            e.fence()
            act_norm(e, acc, a, y)
            act_split_first(e)
            for m in range(KD):
                t = acc.next("act")
                wait_filled(e, t)
                e.eng.activation(halves(pproj[:, m, :]), pair(t.s), ACT.Copy).then_inc(copied["act"], 1)
                e.eng.wait_ge(h_new, e.adds + m + 1)
                act_high(e, h[:, m, :], hh_[:, m, :], xh_ready)
            e.adds += KD
            e.parts += KD
            act_dense_split(e, acc, KD, lambda m: y[:, m, :], lambda m: ACT.Sigmoid)
            e.fence()
            act_norm(e, acc, a, y)

        def dve_layer_end(e, acc, layer):
            dve_split_first(e)
            dve_split_rhs(e, tiles_of(y), tiles_of(yh), tiles_of(y))
            dve_dense_split(e, KD)
            acc.skip(KD)
            e.fence()
            dve_split_first(e)
            dve_norm(e, acc, a, a, layer, "g_mix_post", True)
            dve_pre_norm(e, acc, layer, "g_ffn_pre")
            dve_up(e, acc, layer)
            e.fence()
            dve_down(e, acc)
            e.fence()
            dve_split_first(e)
            dve_norm(e, acc, a, a, layer, "g_ffn_post", True)
            dve_split_rhs(e, tiles_of(h), tiles_of(hh_), tiles_of(hl_))
            dve_dense_split(e, KD)
            acc.skip(KD)
            for m in range(KD):
                e.eng.wait_ge(*acc.next("act").out)
                e.eng.tensor_tensor(a[:, m, :], pproj[:, m, :], y[:, m, :], ALU.mult)
            e.fence()
            dve_norm(e, acc, a, a, layer, "g_ple", True)

        def sp_layer_end(ld, at, down_stage):
            sp_dense_split(ld, KD, at + KD)
            at += KD + 2
            sp_up(ld, at)
            at += 2 * FT
            sp_down(ld, at + KD)
            at += KD + 1
            sp_split_first(ld)
            for s in (pe_stage, act_stage, dve_stage):
                ld.sp.wait_ge(s, down_stage)
            for j in range(2):
                ld.sp.dma_start(plew[:, j], A["w8"][ld.row + RAW + j].rearrange("p (k n) -> p k n", k=KD)).then_inc(pw_in, 16)
            sp_dense_split(ld, KD, at + 2 * KD)
            ld.row += 2
            return at + 2 * KD + 1

        _c[0] = mixer_free

        def heads(at, n=T):
            return cut(at, HH * n).rearrange("p (h t) -> p h t", h=HH)

        qh, kh, bh, gh = (heads(take(HH * T)) for _ in range(4))
        vh = cut(take(4 * 512), 4 * 512).rearrange("p (i n) -> p i n", i=4)
        vhs = cut(take(512), 512)
        s0_at = take(NB * HH * P)
        s0 = cut(s0_at, NB * HH * P).rearrange("p (b h v) -> p b h v", b=NB, h=HH)
        sp_state = cut(take(HH * P), HH * P).rearrange("p (h v) -> p h v", h=HH)
        att_at = take(HH * NCL * P)
        att = cut(att_at, HH * NCL * P).rearrange("p (u t) -> p u t", t=CL)
        att_s = cut(take(HH * NS), HH * NS).rearrange("p (h t) -> p h t", h=HH)
        assert _c[0] <= ARENA, _c[0]
        ex = a_sb[:, 0:HH * T].rearrange("p (h t) -> p h t", h=HH)
        qe = a_sb[:, HH * T:HH * T + HH * HALF].rearrange("p (h t) -> p h t", h=HH)
        kt = a_sb[:, HH * T:HH * T + 2048].rearrange("p (u d) -> p u d", d=P)
        kt_s = rstd[0:NS, 0:HH * P].rearrange("p (h d) -> p h d", h=HH)
        ke = y_sb[:, 0:HH * T].rearrange("p (h t) -> p h t", h=HH)
        lv_tmp = y_sb[:, HH * T:HH * T + 1024]
        lv_tmp_s = y_sb[0:NS, HH * T + 1024:HH * T + 1024 + HH * 32]
        vx = y_sb[0:NS, 0:HH * NB * P].rearrange("p (h b v) -> p h b v", h=HH, b=NB)
        lbt = [small[:, 16 + 4 * i:20 + 4 * i] for i in range(10)]

        def pe_proj_c(e, acc):
            e.eng.wait_ge(x_new, KD * (e.pre + 1))
            e.pre += 1
            pe_value_rows(e, acc, 0, y)
            pe_value_rows(e, acc, 4, y)
            pe_dense_split(e, acc, 20, (a, y), off=2)

        def act_proj_c(e, acc):
            act_value_rows(e, acc, vh, vhs)
            for n in range(2):
                act_split_slab(e, n, None, off=2)
            act_value_rows(e, acc, vt, vs)
            act_split_slab(e, 2, acc.n, off=2)
            dst = [z[:, m, :] for z, n in ((qh, 4), (kh, 4), (gh, 4), (zqk, 8)) for m in range(n)]
            act_dense_split(e, acc, 20, lambda m: dst[m],
                            lambda m: ACT.Sigmoid if m // 4 == 1 else ACT.Silu if m // 4 == 2 else ACT.Copy, off=2)

        def dve_proj_c(e, acc):
            v, do = e.eng, e.st.do
            tt = v.tensor_tensor
            m, e0, e1, lb, oml, t0, t1, t2 = lbt[:8]
            a0, a1 = (vec[:, NVEC + VEC[x]:NVEC + VEC[x] + 4] for x in ("lb0", "lb1"))
            do(tt(m, a0, a1, ALU.max))
            do(tt(e0, a0, m, ALU.subtract))
            do(tt(e1, a1, m, ALU.subtract))
            dve_exp(e, e0, e0, t0, t1, t2)
            dve_exp(e, e1, e1, t0, t1, t2)
            do(tt(m, e0, e1, ALU.add))
            do(v.reciprocal(m, m))
            do(tt(e0, e0, m, ALU.mult))
            do(tt(e1, e1, m, ALU.mult))
            do(tt(lb, e0, e1, ALU.add))
            do(tt(lb, lb, e0, ALU.subtract))
            do(v.tensor_scalar(oml, lb, -1.0, 1.0, ALU.mult, ALU.add))
            for n in range(2):
                dve_split_slab(e, n, off=2)
            acc.skip(10)
            v.wait_ge(acc_ready, acc.n)
            dve_split_rhs(e, tiles_of(y), tiles_of(a), tiles_of(y))
            dve_split_slab(e, 2, off=2)
            for m in range(20):
                if m + AHEAD < 20:
                    dve_split_slab(e, m + AHEAD, off=2)
                t = acc.next("act")
                if m // 4 != 1:
                    continue
                i = m - 4
                v.wait_ge(*t.out)
                do(v.tensor_scalar(bh[:, i, :], kh[:, i, :], oml[:, i:i + 1], lb[:, i:i + 1], ALU.mult, ALU.add))
                do(v.tensor_scalar(kh[:, i, :], bh[:, i, :], -1.0, 1.0, ALU.mult, ALU.add))

        def sp_proj_c(ld, n):
            for j in range(4):
                ld.load(j, n + 5)
            for j in range(4):
                ld.load(4 + j, n + 10)
            sp_split_first(ld)
            sp_dense_split(ld, 20, n + 30)

        lf_ready, dg_ready, ex_ready, exa_ready, qk_ready, lv_ready, kk_ready, kt_ready, ktc_ready = (
            sem(x) for x in ("lf_ready", "dg_ready", "ex_ready", "exa_ready", "qk_ready", "lv_ready", "kk_ready",
                             "kt_ready", "ktc_ready"))
        st_mm, st_new, vx_ready, sk_mm, sk_new, os_ready, oc_ready, osq_ready, ors_ready = (
            sem(x) for x in ("st_mm", "st_new", "vx_ready", "sk_mm", "sk_new", "os_ready", "oc_ready", "osq_ready", "ors_ready"))
        hg_in = sem("hg_in")

        def pe_hgrn(e):
            pe = e.eng
            for u in range(16):
                hh, c = divmod(u, NCL)
                pe.matmul(psum[:, u // 4, (u % 4) * P:(u % 4 + 1) * P], kh[:, hh, c * CL:(c + 1) * CL],
                          qh[:, hh, c * CL:(c + 1) * CL], start=True, stop=True)
            for hh in range(HH):
                last = pe.matmul(psum[0:NS, 4, hh * NS:(hh + 1) * NS], kh[:, hh, TP:T], qh[:, hh, TP:T],
                                 start=True, stop=True)
            last.then_inc(dg_ready, 1)
            for i, w in enumerate(LEVELS):
                pe.wait_ge(qk_ready, i + 1)
                b0 = 5 if i % 2 == 0 else 0
                for u in range(16):
                    hh, c = divmod(u, NCL)
                    last = pe.matmul(psum[:, b0 + u // 8, (u % 8) * 64:(u % 8 + 1) * 64], ke[:, hh, c * CL:(c + 1) * CL],
                                     qe[:, hh, c * 64:(c + 1) * 64], start=True, stop=True)
                if w <= TS // 2:
                    for hh in range(HH):
                        last = pe.matmul(psum[0:NS, b0 + 2, hh * 32:(hh + 1) * 32], ke[:, hh, TP:T],
                                         qe[:, hh, 256:288], start=True, stop=True)
                last.then_inc(lv_ready, 1)
            pe.wait_ge(kk_ready, 1)
            for u in range(16):
                hh, c = divmod(u, NCL)
                pe.transpose(psum[:, u // 4, (u % 4) * P:(u % 4 + 1) * P], ke[:, hh, c * CL:(c + 1) * CL], ident)
            for hh in range(HH):
                last = pe.transpose(psum[0:NS, 4, hh * P:(hh + 1) * P], ke[:, hh, TP:T], ident)
            last.then_inc(kt_ready, 1)
            pe.wait_ge(ktc_ready, 1)
            for c in range(NCL):
                for hh in range(HH):
                    last = pe.matmul(psum[:, 5 + c % 2, hh * P:(hh + 1) * P], kt[:, NCL * hh + c, :],
                                     vh[:, c, hh * P:(hh + 1) * P], start=True, stop=True)
                last.then_inc(st_mm, 1)
                if c:
                    pe.wait_ge(st_new, c)
                for hh in range(HH):
                    o = psum[:, hh, c * CL:(c + 1) * CL]
                    last = pe.matmul(o, vh[:, c, hh * P:(hh + 1) * P], att[:, NCL * hh + c, :], start=True, stop=(c == 0))
                    if c:
                        last = pe.matmul(o, sp_state[:, hh, :], qh[:, hh, c * CL:(c + 1) * CL], start=False, stop=True)
                last.then_inc(os_ready, 1)
            pe.wait_ge(hg_in, 16)
            for hh in range(HH):
                for b in range(NB):
                    o = psum[:, 4, hh * NS + b * TS:hh * NS + (b + 1) * TS]
                    pe.matmul(o, vhs[0:NS, hh * P:(hh + 1) * P], att_s[0:NS, hh, b * TS:(b + 1) * TS],
                              start=True, stop=False)
                    last = pe.matmul(o, s0[:, b, hh, :], qh[:, hh, TP + b * TS:TP + (b + 1) * TS],
                                     start=False, stop=True)
            last.then_inc(os_ready, 1)
            pe.wait_ge(vx_ready, 1)
            pe.wait_ge(st_new, NCL)
            for hh in range(HH):
                b0 = 5 if hh % 2 == 0 else 0
                if hh == 1:
                    pe.wait_ge(oc_ready, 1)
                if hh >= 2:
                    pe.wait_ge(sk_new, hh - 1)
                for g in range(2):
                    last = pe.matmul(psum[:, b0 + g, :], kt_s[:, hh, :],
                                     vx[:, hh, 4 * g:4 * g + 4, :], start=True, stop=True)
                last.then_inc(sk_mm, 1)
            pe.wait_ge(osq_ready, 1)
            pe.wait_ge(sk_new, HH)
            for hh in range(HH):
                for half in range(2):
                    last = pe.matmul(psum[:, 2 * hh + half, 0:HALF], ones, bh[:, hh, half * HALF:(half + 1) * HALF],
                                     start=True, stop=True)
            last.then_inc(ors_ready, 1)

        def act_hgrn(e):
            act = e.eng
            act.preload_act_table_set("natural_log_exp_and_others")
            act.activation(bh, bh, ACT.Ln).then_inc(lf_ready, 1)
            for i, w in enumerate(LEVELS):
                act.wait_ge(ex_ready, i + 1)
                x = ex if w <= TS // 2 else ex[:, :, 0:TP]
                act.activation(x, x, ACT.Exp).then_inc(exa_ready, 1)
            act.wait_ge(qk_ready, len(LEVELS))
            act.activation(ex, bh, ACT.Exp)
            act.wait_ge(ex_ready, len(LEVELS) + 1)
            act.activation(ke, ke, ACT.Exp).then_inc(exa_ready, 1)
            act.wait_ge(kt_ready, 1)
            act.activation(kt.rearrange("p (b u) d -> p b (u d)", b=4), psum[:, 0:4, :], ACT.Copy)
            act.activation(kt_s, psum[0:NS, 4, :].rearrange("p (h d) -> p h d", h=HH), ACT.Copy).then_inc(ktc_ready, 1)
            act.wait_ge(os_ready, NCL + 1)
            act.activation(kh[:, :, 0:TP], psum[:, 0:4, :], ACT.Copy)
            act.activation(kh[:, :, TP:T], psum[:, 4, 0:HH * NS].rearrange("p (h t) -> p h t", h=HH), ACT.Copy)\
               .then_inc(oc_ready, 1)
            act.wait_ge(oc_ready, 1)
            act.activation(bh, kh, ACT.Square).then_inc(osq_ready, 1)
            act.wait_ge(ors_ready, 1)
            e.st.do(act.activation(ex.rearrange("p h (a n) -> p (h a) n", a=2), psum[:, :, 0:HALF], ACT.Ln,
                                   scale=1.0 / P, bias=eps_col))
            act.activation(ex, ex, ACT.Exp, scale=-0.5).then_inc(exa_ready, 1)

        def dve_hgrn(e):
            v, do = e.eng, e.st.do
            tt = v.tensor_tensor
            L = LCON[1]
            do(v.memset(ke, 0.0))
            v.wait_ge(lf_ready, 1)
            for hh in range(HH):
                do(v.tensor_tensor_scan(out=bh[:, hh, :], data0=lcon[:, L["reset"]:L["reset"] + T], data1=bh[:, hh, :],
                                        initial=0.0, op0=ALU.mult, op1=ALU.add))

            def add_diagonal():
                v.wait_ge(dg_ready, 1)
                do(tt(att, psum[:, 0:4, :].rearrange("p b n -> p (b n)").rearrange("p (u t) -> p u t", t=CL),
                      ident.unsqueeze(1).to_broadcast([P, 16, CL]), ALU.mult))
                do(tt(att_s[0:NS], psum[0:NS, 4, 0:HH * NS].rearrange("p (h t) -> p h t", h=HH),
                      ident[0:NS, 0:NS].unsqueeze(1).to_broadcast([NS, HH, NS]), ALU.mult))

            def add_level(i):
                w = LEVELS[i]
                b0 = 5 if i % 2 == 0 else 0
                mask = lcon[:, L["level"] + 64 * i:L["level"] + 64 * (i + 1)]
                v.wait_ge(lv_ready, i + 1)
                do(tt(lv_tmp.rearrange("p (u j) -> p u j", j=64),
                      psum[:, b0:b0 + 2, :].rearrange("p b n -> p (b n)").rearrange("p (u j) -> p u j", j=64),
                      mask.unsqueeze(1).to_broadcast([P, 16, 64]), ALU.mult))
                right = att.rearrange("p u (n x) -> p (u n) x", x=2 * w)[:, :, w:]
                do(tt(right, right, lv_tmp.rearrange("p (n x) -> p n x", x=w), ALU.add))
                if w <= TS // 2:
                    do(tt(lv_tmp_s.rearrange("p (h j) -> p h j", j=32),
                          psum[0:NS, b0 + 2, 0:HH * 32].rearrange("p (h j) -> p h j", j=32),
                          mask[0:NS, 0:32].unsqueeze(1).to_broadcast([NS, HH, 32]), ALU.mult))
                    right = att_s[0:NS].rearrange("p h (n x) -> p (h n) x", x=2 * w)[:, :, w:]
                    do(tt(right, right, lv_tmp_s.rearrange("p (n x) -> p n x", x=w), ALU.add))

            for i, w in enumerate(LEVELS):
                cols = T if w <= TS // 2 else TP

                def blocks(z):
                    return z[:, :, 0:cols].rearrange("p h (n x) -> p h n x", x=2 * w)

                bb, xx = blocks(bh), blocks(ex)
                ref = bb[:, :, :, w - 1:w].to_broadcast([P, HH, cols // (2 * w), w])
                do(tt(xx[:, :, :, w:], bb[:, :, :, w:], ref, ALU.subtract))
                tt(xx[:, :, :, 0:w], ref, bb[:, :, :, 0:w], ALU.subtract).then_inc(ex_ready, 1)
                if i:
                    add_level(i - 1)
                else:
                    add_diagonal()
                v.wait_ge(exa_ready, i + 1)
                do(tt(qe[:, :, 0:cols // 2].rearrange("p h (n x) -> p h n x", x=w), blocks(qh)[:, :, :, w:],
                      xx[:, :, :, w:], ALU.mult))
                last = tt(blocks(ke)[:, :, :, 0:w], blocks(kh)[:, :, :, 0:w], xx[:, :, :, 0:w], ALU.mult)
                last.then_inc(qk_ready, 1)
                v.wait_ge(qk_ready, i + 1)
            add_level(len(LEVELS) - 1)
            for z, n, at in ((bh[:, :, 0:TP], CL, 0), (bh[:, :, TP:T], TS, TP)):
                k = (TP if at == 0 else NS) // n
                zz = z.rearrange("p h (n x) -> p h n x", x=n)
                last = tt(ke[:, :, at:at + k * n].rearrange("p h (n x) -> p h n x", x=n),
                          zz[:, :, :, n - 1:n].to_broadcast([P, HH, k, n]), zz, ALU.subtract)
            last.then_inc(ex_ready, 1)
            v.wait_ge(exa_ready, len(LEVELS) + 1)
            do(tt(qh, qh, ex, ALU.mult))
            tt(ke, ke, kh, ALU.mult).then_inc(kk_ready, 1)
            v.wait_ge(ktc_ready, 1)
            blk = con[0:NS, 4 * P:4 * P + NB]
            for hh in range(HH):
                last = tt(vx[:, hh, :, :], vhs[0:NS, hh * P:(hh + 1) * P].unsqueeze(1).to_broadcast([NS, NB, P]),
                          blk.unsqueeze(2).to_broadcast([NS, NB, P]), ALU.mult)
            last.then_inc(vx_ready, 1)
            for c in range(NCL):
                v.wait_ge(st_mm, c + 1)
                if c:
                    v.wait_ge(os_ready, c + 1)
                for hh in range(HH):
                    new = psum[:, 5 + c % 2, hh * P:(hh + 1) * P]
                    if c == 0:
                        last = v.tensor_copy(sp_state[:, hh, :], new)
                    else:
                        last = v.scalar_tensor_tensor(sp_state[:, hh, :], sp_state[:, hh, :],
                                                      ex[:, hh, (c + 1) * CL - 1:(c + 1) * CL], new, ALU.mult, ALU.add)
                last.then_inc(st_new, 1)
                v.wait_ge(st_new, c + 1)
            v.wait_ge(os_ready, NCL + 1)
            for hh in range(HH):
                b0 = 5 if hh % 2 == 0 else 0
                v.wait_ge(sk_mm, hh + 1)
                for b in range(NB):
                    at = TP + (b + 1) * TS - 1
                    last = v.scalar_tensor_tensor(s0[:, b, hh, :], s0[:, b, hh, :], ex[:, hh, at:at + 1],
                                                  psum[:, b0 + b // 4, (b % 4) * P:(b % 4 + 1) * P], ALU.mult, ALU.add)
                last.then_inc(sk_new, 1)
            v.wait_ge(exa_ready, len(LEVELS) + 2)
            g = vec[:, NVEC + VEC["g_hgrn"]:NVEC + VEC["g_hgrn"] + 1]
            f = "p h t -> p (h t)"
            do(v.scalar_tensor_tensor(y_sb[:, 0:HH * T], kh.rearrange(f), g, ex.rearrange(f), ALU.mult, ALU.mult))
            do(tt(y_sb[:, 0:HH * T], y_sb[:, 0:HH * T], gh.rearrange(f), ALU.mult))

        z_t, e_t, s_t, r_t = ([cut(unit_at + (2 * j + i) * 512, 512) for i in range(2)] for j in range(4))
        w_t = [cut(unit_at + 4096, 512), rstd[:, 0:512]]
        assert unit_at + 4096 + 512 <= ARENA
        DUE_C = {"pe": (8, (4, 7, 11, 12, 13, 14)), "act": (8, (8, 9, 10, 11)), "dve": (8, (8, 10, 13, 14))}
        zs_ready, zc_ready, nz_ready, l_ready, sp_ready, tt_ready, d_ready, w_ready, ow_ready, ocp_ready = (
            sem(x) for x in ("zs_ready", "zc_ready", "nz_ready", "l_ready", "sp_ready", "tt_ready", "d_ready", "w_ready",
                             "ow_ready", "ocp_ready"))
        SBU = [(hh, j) for hh in range(NH) for j in (3, 2, 1, 0)]

        def pe_sb_prompt(e):
            pe = e.eng
            samples = [pe_sample_pair(e, 1, i) for i in range(NPAIR)]
            for u in range(len(SBU) + 2):
                if u < len(SBU):
                    hh, j = SBU[u]
                    r0, c, n = 64 * (hh % 2), hh // 2, TP - P * j
                    if u >= 2:
                        pe.wait_ge(zc_ready, u - 1)
                    pe.matmul(psum[:, u % 2, 0:n], zqk[r0:r0 + 64, 4 + c, j * P:(j + 1) * P], zqk[r0:r0 + 64, c, j * P:TP],
                              start=True, stop=True).then_inc(zs_ready, 1)
                if 1 <= u <= len(SBU):
                    hh, j = SBU[u - 1]
                    n = TP - P * j
                    b = (u - 1) % 2
                    pe.wait_ge(sp_ready, u)
                    if u >= 3:
                        pe.wait_ge(d_ready, u - 2)
                    last = pe.matmul(psum[:, 2 + b, 0:P], tri, s_t[b][:, 0:P], start=True, stop=True)
                    if j < 3:
                        pe.matmul(psum[:, 2 + b, P:n], tri, s_t[b][:, P:n], start=True, stop=False)
                        last = pe.matmul(psum[:, 2 + b, P:n], ones, r_t[b][:, P:n], start=False, stop=True)
                    last.then_inc(tt_ready, 1)
                if u >= 2:
                    hh, j = SBU[u - 2]
                    r0, c, n = 64 * (hh % 2), hh // 2, TP - P * j
                    pe.wait_ge(w_ready, u - 1)
                    if hh % 2 == 0 and j == 3 and c >= 1:
                        pe.wait_ge(ocp_ready, c)
                    pe.matmul(psum[r0:r0 + 64, 4, j * P:TP], vt[:, j, hh * HD:(hh + 1) * HD], w_t[u % 2][:, 0:n],
                              start=(j == 3), stop=True, skip_group_check=True).then_inc(ow_ready, 1)
                between(samples, u, len(SBU) + 1, DUE_C["pe"])

        def act_sb_prompt(e):
            act = e.eng
            act.preload_act_table_set("natural_log_exp_and_others")

            def copy_out(c):
                act.wait_ge(ow_ready, 8 * (c + 1))
                act.activation(y[:, 4 + c, 0:TP], psum[:, 4, :], ACT.Copy).then_inc(ocp_ready, 1)

            samples = [act_sb_sample(e, i) for i in range(NPAIR)]
            for u in range(len(SBU) + 2):
                if 1 <= u <= len(SBU):
                    n, b = TP - P * SBU[u - 1][1], (u - 1) % 2
                    act.wait_ge(nz_ready, u)
                    e.st.do(act.activation(e_t[b][:, 0:n], e_t[b][:, 0:n], ACT.Exp))
                    act.activation(e_t[b][:, 0:n], e_t[b][:, 0:n], ACT.Ln, bias=one_col).then_inc(l_ready, 1)
                if u >= 2:
                    n, b = TP - P * SBU[u - 2][1], u % 2
                    act.wait_ge(d_ready, u - 1)
                    if u >= 4:
                        act.wait_ge(ow_ready, u - 3)
                    act.activation(w_t[b][:, 0:n], w_t[b][:, 0:n], ACT.Exp).then_inc(w_ready, 1)
                if u < len(SBU):
                    n, b = TP - P * SBU[u][1], u % 2
                    act.wait_ge(zs_ready, u + 1)
                    if u >= 2:
                        act.wait_ge(d_ready, u - 1)
                    act.activation(z_t[b][:, 0:n], psum[:, b, 0:n], ACT.Copy, scale=ATT_SCALE).then_inc(zc_ready, 1)
                if u >= 9 and (u - 9) % 8 == 0:
                    copy_out((u - 9) // 8)
                between(samples, u, len(SBU) + 1, DUE_C["act"])

        def dve_sb_prompt(e):
            v, do = e.eng, e.st.do
            tt = v.tensor_tensor
            dve_queries(e)
            samples = [dve_sb_sample(e, i) for i in range(NPAIR)]
            causal = lcon[:, LCON[1]["causal"]:LCON[1]["causal"] + P]
            for u in range(len(SBU) + 2):
                if u >= 2:
                    n, b = TP - P * SBU[u - 2][1], u % 2
                    v.wait_ge(tt_ready, u - 1)
                    if u >= 4:
                        v.wait_ge(ow_ready, u - 3)
                    tt(w_t[b][:, 0:n], z_t[b][:, 0:n], psum[:, 2 + b, 0:n], ALU.subtract).then_inc(d_ready, 1)
                if 1 <= u <= len(SBU):
                    j, b = SBU[u - 1][1], (u - 1) % 2
                    n = TP - P * j
                    v.wait_ge(l_ready, u)
                    if u >= 3:
                        v.wait_ge(tt_ready, u - 2)
                    v.scalar_tensor_tensor(s_t[b][:, 0:n], z_t[b][:, 0:n], 0.0, e_t[b][:, 0:n], ALU.max, ALU.add)\
                     .then_inc(sp_ready, 1)
                    v.wait_ge(sp_ready, u)
                    if u >= 2:
                        v.wait_ge(tt_ready, u - 1)
                    if j:
                        r = r_t[1 - b]
                        do(v.tensor_copy(r[:, P:2 * P], s_t[b][:, 0:P]))
                        if j < 3:
                            do(tt(r[:, 2 * P:n + P], s_t[b][:, P:n], r_t[b][:, P:n], ALU.add))
                if u < len(SBU):
                    n, b = TP - P * SBU[u][1], u % 2
                    v.wait_ge(zc_ready, u + 1)
                    do(tt(z_t[b][:, 0:P], z_t[b][:, 0:P], causal, ALU.add))
                    v.scalar_tensor_tensor(e_t[b][:, 0:n], z_t[b][:, 0:n], -1.0, z_t[b][:, 0:n], ALU.mult, ALU.min)\
                     .then_inc(nz_ready, 1)
                between(samples, u, len(SBU) + 1, DUE_C["dve"])

        def act_sb_sample(e, i):
            act, z, x = e.eng, wz, we
            act.wait_ge(k_used, NB + 2 * i + 2)
            act.activation(z[:, 0:PAST].rearrange("p (a n) -> p a n", a=2), psum[:, 5:7, :], ACT.Copy,
                           scale=ATT_SCALE).then_inc(z_copied, 1)
            yield
            act.wait_ge(neg_ready, i + 1)
            e.st.do(act.activation(x, x, ACT.Exp))
            act.activation(x, x, ACT.Ln, bias=one_col).then_inc(soft_ready, 1)
            yield
            act.wait_ge(sub_ready, i + 1)
            act.activation(z, z, ACT.Exp).then_inc(sw_ready, 1)
            yield
            act_turned(e, NPAIR + i)
            yield

        def dve_sb_sample(e, i):
            v, do, z, x = e.eng, e.st.do, wz, we
            tt, stt = v.tensor_tensor, v.scalar_tensor_tensor
            v.wait_ge(k_used, NB + 2 * i + 2)
            v.wait_ge(wt_full, NPAIR + i)
            new = lcon[:, LCON[1]["new"] + NS * i:LCON[1]["new"] + NS * (i + 1)]
            do(stt(z[:, PAST:KEYS], s_new, ATT_SCALE, new, ALU.mult, ALU.add))
            v.wait_ge(z_copied, i + 1)
            stt(x, z, -1.0, z, ALU.mult, ALU.min).then_inc(neg_ready, 1)
            yield
            v.wait_ge(soft_ready, i + 1)
            do(stt(x, z, 0.0, x, ALU.max, ALU.add))
            do(v.tensor_tensor_scan(out=x[:, ::-1], data0=one_col.to_broadcast([P, KEYS]), data1=x[:, ::-1], initial=0.0,
                                    op0=ALU.mult, op1=ALU.add))
            tt(z, z, x, ALU.subtract).then_inc(sub_ready, 1)
            yield
            yield from dve_outputs(e, i, NPAIR + i, None)

        y_stored = sem("y_stored")

        @block.sync
        def _(sp):
            sp.dma_start(con[:, :], A["con"]).then_inc(con_in, 16)
            sp.dma_start(small[:, :], A["small"]).then_inc(con_in, 16)
            for k in range(KD):
                sp.dma_start(h[:, k], A["x"].rearrange("(k p) t -> p k t", p=P)[:, k]).then_inc(x_in[k], 16)
            sp.dma_start(vec[:, :], A["vec"]).then_inc(vec_in, 16)
            sp.dma_start(lcon[:, :], A["lcon"][0]).then_inc(lcon_in, 16)
            for dst, name in S5_LOADS:
                sp.dma_start(dst, A[name]).then_inc(s5_in, 16)
            ld = Loader(sp)
            sp_proj_a(ld, 1)
            sp_s5_states(ld)
            at = 1 + 29 + 12 + 8
            ld.load(0, at + 2)
            ld.load(1, at + 4)
            at += 4
            sp_split_first(ld)
            sp.dma_start(pages[0:1, :], A["pages"]).then_inc(pages_in, 16)
            sp.wait_ge(pages_in, 16)
            for s in (pe_stage, act_stage, dve_stage):
                sp.wait_ge(s, 4)
            sp_stream(sp, A["moba_k"], A["moba_v"], 0)
            at = sp_layer_end(ld, at, 8)
            for s in (pe_stage, act_stage, dve_stage):
                sp.wait_ge(s, 5)
            sp.dma_start(lcon[:, :], A["lcon"][1]).then_inc(lcon_in, 16)
            sp_proj_c(ld, at + 1)
            at += 1 + 30
            sp_split_first(ld)
            for s in (pe_stage, act_stage, dve_stage):
                sp.wait_ge(s, 11)
            sp.wait_ge(stored, 16 * 11)
            sp_stream(sp, A["sb_k"], A["sb_v"], 1)
            sp_layer_end(ld, at, 15)
            for k in range(KD):
                sp.wait_ge(h_new, 5 * KD + k + 1)
                sp.dma_start(A["o_h"].rearrange("(k p) t -> p k t", p=P)[:, k], h[:, k, :]).then_inc(y_stored, 16)
            sp.wait_ge(y_stored, 16 * KD)

        @block.gpsimd
        def _(eng):
            def ended(stage):
                for s in (pe_stage, act_stage, dve_stage):
                    eng.wait_ge(s, stage)

            def store(dst, src):
                eng.dma_start(dst, src).then_inc(stored, 16)
                eng_stores[0] += 16

            eng_stores = [0]
            ended(3)
            store(A["o_mk"], zqk[:, 4:8, :])
            store(A["o_mv"][0:TP].rearrange("(i p) n -> p i n", p=P), vt)
            store(A["o_mv"][TP:T], vs[0:NS, :])
            store(A["o_s5r"], s5o[0])
            store(A["o_s5i"], s5o[1])
            ended(5)
            eng.dma_start(fst, A["ffn_st"][0]).then_inc(fst_in, 16)
            ended(7)
            store(A["o_ffn"][0], fo)
            ended(8)
            eng.dma_start(ptile, A["p"][0].rearrange("(k p) t -> p k t", p=P)).then_inc(pt_in, 16)
            ended(10)
            eng.wait_ge(stored, 16 * 6)
            eng.dma_start(s0, A["hgrn_st"]).then_inc(hg_in, 16)
            store(A["o_sk"], zqk[:, 4:8, :])
            store(A["o_sv"][0:TP].rearrange("(i p) n -> p i n", p=P), vt)
            store(A["o_sv"][TP:T], vs[0:NS, :])
            ended(11)
            store(A["o_hg"][:, 0:HH, :], sp_state)
            store(A["o_hg"][:, HH:, :].rearrange("p (b h) v -> p b h v", b=NB), s0)
            ended(12)
            eng.wait_ge(stored, 16 * 11)
            eng.dma_start(fst, A["ffn_st"][1]).then_inc(fst_in, 16)
            ended(14)
            store(A["o_ffn"][1], fo)
            ended(15)
            eng.dma_start(ptile, A["p"][1].rearrange("(k p) t -> p k t", p=P)).then_inc(pt_in, 16)
            eng.wait_ge(stored, eng_stores[0])

        @block.scalar
        def _(eng):
            e, acc = Engine(eng, act_stage, act_step), Acc()
            eng.wait_ge(con_in, 32)
            act_norm(e, acc, h, a, arrive=x_in)
            e.fence()
            act_proj_a(e, acc)
            e.fence()
            act_s5_states(e, acc)
            e.fence()
            act_s5_out(e, acc)
            act_glu(e, acc)
            e.fence()
            act_moba_prompt(e)
            e.fence()
            act_layer_end(e, acc, 0)
            act_pre_norm(e, acc)
            eng.wait_ge(stored, 16 * 6)
            act_proj_c(e, acc)
            e.fence()
            act_hgrn(e)
            e.fence()
            eng.wait_ge(stored, 16 * 11)
            act_sb_prompt(e)
            e.fence()
            act_layer_end(e, acc, 1)
            e.fence()

        @block.vector
        def _(eng):
            e, acc = Engine(eng, dve_stage, dve_step), Acc()
            eng.wait_ge(con_in, 32)
            eng.wait_ge(vec_in, 16)
            dve_norm(e, acc, h, a, 0, "g_mix_pre")
            e.fence()
            eng.wait_ge(lcon_in, 16)
            dve_s5_params(e)
            dve_s5_tables(e)
            dve_proj_a(e, acc)
            e.fence()
            dve_s5_states(e, acc)
            e.fence()
            for _ in s5_out_tiles(acc):
                pass
            dve_glu(e, acc)
            e.fence()
            dve_moba_prompt(e)
            e.fence()
            dve_layer_end(e, acc, 0)
            dve_norm(e, acc, h, y, 1, "g_mix_pre", ready=x_new)
            eng.wait_ge(stored, 16 * 6)
            dve_proj_c(e, acc)
            e.fence()
            eng.wait_ge(lcon_in, 32)
            dve_hgrn(e)
            e.fence()
            eng.wait_ge(stored, 16 * 11)
            dve_sb_prompt(e)
            e.fence()
            dve_layer_end(e, acc, 1)
            e.fence()

        @block.tensor
        def _(eng):
            e, acc = Engine(eng, pe_stage), Acc()
            eng.wait_ge(con_in, 32)
            pe_norm(e, acc, a)
            e.fence()
            pe_proj_a(e, acc)
            e.fence()
            pe_s5_states(e, acc)
            e.fence()
            pe_s5_out(e, acc)
            eng.wait_ge(copied["act"], acc.count["act"])
            pe_glu(e, acc)
            e.fence()
            pe_moba_prompt(e)
            e.fence()
            pe_layer_end(e, acc)
            pe_norm(e, acc, a)
            pe_proj_c(e, acc)
            e.fence()
            pe_hgrn(e)
            e.fence()
            pe_sb_prompt(e)
            e.fence()
            pe_layer_end(e, acc)
            e.fence()


def tiles(v):
    return np.asarray(v).reshape(-1, P).T


def shape_constants():
    con = np.zeros((P, NCON), np.float32)
    r = np.arange(P)
    con[:, CON["ident"]:CON["ident"] + P] = np.eye(P)
    con[:, CON["ones"]:CON["ones"] + P] = 1.0
    for hd in (0, HD):
        for i in range(8):
            con[hd + i + 8, CON["rot"] + hd + i] = -1.0
            con[hd + i, CON["rot"] + hd + i + 8] = 1.0
    con[:, CON["tri"]:CON["tri"] + P] = r[:, None] >= r[None, :]
    con[:, 4 * P:4 * P + NB] = r[:, None] // TS == np.arange(NB)[None, :]
    lcon = np.zeros((2, P, NLCON), np.float32)
    pos = np.concatenate([np.arange(TP), np.tile(PAST + np.arange(TS), NB)]).astype(np.float32)
    inv = (np.float32(500000.0) ** (-np.arange(8, dtype=np.float32) / np.float32(8))).astype(np.float32)
    ang = (pos[None, :] * inv[:, None]).astype(np.float32)
    c = LCON[0]
    lcon[0, :, c["cos"]:c["cos"] + T] = 1.0
    for hd in (0, 8, HD, HD + 8):
        lcon[0, hd:hd + 8, c["cos"]:c["cos"] + T] = np.cos(ang)
        lcon[0, hd:hd + 8, c["sin"]:c["sin"] + T] = np.sin(ang)
    lcon[0, :, c["causal"]:c["causal"] + P] = np.where(r[None, :] <= r[:, None], 0, NEG)
    kb, kt = np.divmod(np.arange(NS), TS)
    qs, qt = r // 16 % 2, r % TS
    same = kb[None, None, :] == 2 * np.arange(NB // 2)[None, :, None] + qs[:, None, None]

    def new(ok):
        return np.where(same & ok[:, None, :], 0, NEG).reshape(P, -1)

    lcon[0, :, c["new"]:c["new"] + NB // 2 * NS] = new(kt[None, :] <= qt[:, None])
    c = LCON[1]
    t = np.arange(T)
    lcon[1, :, c["reset"]:c["reset"] + T] = np.where(t < TP, t % CL != 0, t % TS != 0)
    for i, w in enumerate(LEVELS):
        j = np.arange(64)
        ok = (r[:, None] // (2 * w) == j[None, :] // w) & (r[:, None] % (2 * w) < w)
        lcon[1, :, c["level"] + 64 * i:c["level"] + 64 * (i + 1)] = ok
    lcon[1, :, c["causal"]:c["causal"] + P] = np.where(r[:, None] < r[None, :], 0, NEG)
    lcon[1, :, c["new"]:c["new"] + NB // 2 * NS] = new(kt[None, :] < qt[:, None])
    small = np.zeros((P, 64), np.float32)
    small[:, 0] = EPS
    small[:, 1] = 1.0
    small[:, 2] = np.pi / 2
    return con, lcon, small


def slabs_of(w):
    k, n = w.shape
    return w.reshape(k // P, P, n // P, P).transpose(2, 1, 0, 3).reshape(n // P, P, -1)


def lay_out(x):
    A = {}
    A["con"], A["lcon"], A["small"] = shape_constants()
    A["x"] = np.concatenate([x["x_prompt"][0], x["x_sample"].reshape(NS, D)]).T
    A["p"] = np.stack([np.concatenate([x["p_prompt"][i, 0], x["p_sample"][i].reshape(NS, PLE)]).T for i in range(DEPTH)])
    vec = np.zeros((P, DEPTH * NVEC), np.float32)
    for i in range(DEPTH):
        parts = {n: x[n][i] for n in ("g_mix_pre", "g_mix_post", "g_ffn_pre", "g_ffn_post", "g_ple")}
        for j in range(3):
            parts[f"conv{j}"] = x["w_ffn_conv"][i, j]
        parts["conv_b"] = x["b_ffn_conv"][i]
        if i == 0:
            parts["b_glu"] = x["s5_b_glu"][0]
        else:
            parts["lb0"], parts["lb1"], parts["g_hgrn"] = x["hgrn_lb"][0], x["hgrn_lb"][1], x["g_hgrn_norm"][0]
        for n, v in parts.items():
            v = tiles(v)
            vec[:, i * NVEC + VEC[n]:i * NVEC + VEC[n] + v.shape[1]] = v
    A["vec"] = vec

    def pairs(v):
        return np.moveaxis(v.reshape(GP, P, *v.shape[2:]), 0, 1)

    A["s5_ar"], A["s5_ai"] = pairs(x["s5_a_re"][0]), pairs(x["s5_a_im"][0])
    A["s5_ldt"] = pairs(np.repeat(x["s5_log_dt"][0][:, None], SP_, 1))
    A["s5_bc"] = np.concatenate([pairs(v).reshape(P, -1) for v in (
        x["s5_b_re"][0], x["s5_b_im"][0], x["s5_c_re"][0].transpose(0, 2, 1), x["s5_c_im"][0].transpose(0, 2, 1))], 1)
    A["s5_d"] = x["s5_d"][0].T
    A["s5_st"] = np.concatenate([pairs(x[n][0].transpose(1, 2, 0)).reshape(P, -1) for n in ("state_s5_re", "state_s5_im")], 1)
    A["hgrn_st"] = x["state_hgrn"][0].transpose(2, 0, 1, 3)
    A["ffn_st"] = x["state_ffn"].reshape(DEPTH, NB, 2, 2 * FT, P).transpose(0, 4, 3, 1, 2)
    A["pages"] = x["page_table"].reshape(1, -1)
    for n in ("moba", "sb"):
        k = x[f"cache_{n}_k"][0]
        A[f"{n}_k"] = k.reshape(k.shape[0], PAGE, 4, P).transpose(0, 3, 2, 1)
        A[f"{n}_v"] = x[f"cache_{n}_v"][0].reshape(k.shape[0], PAGE, NH * HD)

    def glu_slabs(w, kb):
        s = slabs_of(w)
        return s.reshape(-1, 8 // kb, P, kb * P).transpose(0, 2, 1, 3).reshape(-1, P, KD * P)

    rows, down = [], []
    for i in range(DEPTH):
        if i == 0:
            rows += [slabs_of(x["w_in_a"][0]), glu_slabs(x["s5_w_glu"][0], 4), slabs_of(x["w_out_a"][0])]
            s = rows[0]
            rows[0] = np.concatenate([s[0:4], s[12:16], s[4:12]])
        else:
            s = slabs_of(x["w_in_c"][0])
            rows += [np.concatenate([s[8:12], s[24:28], s[0:8], s[12:16], s[16:24]]), slabs_of(x["w_out_c"][0])]
        s = slabs_of(x["w_ffn_up"][i]).reshape(2, FT, P, -1)
        rows += [s.transpose(1, 0, 2, 3).reshape(2 * FT, P, -1)]
        rows += [slabs_of(x["w_ple_gate"][i]), glu_slabs(x["w_ple_proj"][i], 2)]
        d = slabs_of(x["w_ffn_down"][i])
        down.append(d.reshape(KD, P, 2, DSLAB).transpose(0, 2, 1, 3).reshape(2 * KD, P, DSLAB))
    A["w8"], A["wd"] = np.concatenate(rows), np.concatenate(down)
    return {n: np.ascontiguousarray(v) for n, v in A.items()}


OUTS = {
    "o_h": (D, T), "o_mk": (P, 4, T), "o_mv": (T, 512), "o_s5r": (P, GP, 9), "o_s5i": (P, GP, 9),
    "o_hg": (P, HH * (NB + 1), P), "o_sk": (P, 4, T), "o_sv": (T, 512), "o_ffn": (DEPTH, P, 2 * FT, 2 + 2 * NB),
}


def kernel(**inputs):
    import concourse.bacc as bacc
    from concourse.bass_utils import run_bass_kernel_spmd

    nc = bacc.Bacc("TRN2", target_bir_lowering=False, num_devices=1)
    arrays = lay_out({n: np.asarray(v) for n, v in inputs.items()})
    A = {n: nc.dram_tensor(n, v.shape, mybir.dt.from_np(v.dtype), kind="ExternalInput").ap() for n, v in arrays.items()}
    for n, shape in OUTS.items():
        A[n] = nc.dram_tensor(n, shape, F32, kind="ExternalOutput").ap()
    build(nc, A)
    r = run_bass_kernel_spmd(nc, [arrays], core_ids=[0]).results[0]

    def keys(v, n):
        v = v.transpose(2, 1, 0).reshape(T, NH, HD)
        return v[:TP].reshape(1, 1, TP, NH, HD), v[TP:].reshape(1, NB, TS, NH, HD)

    def vals(v):
        return v[:TP].reshape(1, 1, TP, NH, HD), v[TP:].reshape(1, NB, TS, NH, HD)

    def s5(v):
        v = v.transpose(2, 1, 0).reshape(9, GRP, SP_)
        return v[0].reshape(1, 1, GRP, SP_), v[1:].reshape(1, NB, GRP, SP_)

    hout = r["o_h"].T
    mk, mv, sk, sv = keys(r["o_mk"], 0), vals(r["o_mv"]), keys(r["o_sk"], 0), vals(r["o_sv"])
    sr, si = s5(r["o_s5r"]), s5(r["o_s5i"])
    hg = r["o_hg"].transpose(1, 0, 2)
    ffn = r["o_ffn"].transpose(0, 3, 2, 1).reshape(DEPTH, 2 + 2 * NB, 2 * DFF)
    out = (hout[:TP].reshape(1, TP, D), hout[TP:].reshape(NB, TS, D),
           mk[0], mv[0], sr[0], si[0], hg[:HH].reshape(1, 1, HH, P, P), sk[0], sv[0], ffn[:, None, :2],
           mk[1], mv[1], sr[1], si[1], hg[HH:].reshape(1, NB, HH, P, P), sk[1], sv[1],
           ffn[:, 2:].reshape(DEPTH, NB, 2, 2 * DFF))
    return tuple(np.ascontiguousarray(v) for v in out)
```
